# Optimizing a Trainium2 kernel written in Bass

```python
import math
import jax
import jax.numpy as jnp
from jax import lax
import numpy as np
import jax, jax.numpy as jnp

D_MODEL = 1024
BATCH = 1
SEQ = 512
DEPTH = 1

GRID_W = 64
CTX_LEN = 256
N_MIXERS = 4
D_FF = 4 * D_MODEL
N_MOD = 6
EPS = 1e-6
CONV_W = 3
HG_HEAD_DIM = 128
HG_HEADS = D_MODEL // HG_HEAD_DIM
HG_CHUNK = 32
S5_GROUP = 16
S5_GROUPS = D_MODEL // S5_GROUP
S5_STATE = 64
S5_DT_MIN = 1e-3
S5_DT_MAX = 1e-1
NA_HEADS = 16
NA_HEAD_DIM = D_MODEL // NA_HEADS
NA_ROWS = 8
NA_COLS = 16
NA_STRIP = 2 * NA_COLS


def _layers_of(mixer):
    return len(range(mixer, DEPTH, N_MIXERS))

def rmsnorm(x, g):
    xf = x.astype(jnp.float32)
    y = xf * lax.rsqrt(jnp.mean(xf * xf, axis=-1, keepdims=True) + EPS)
    return (y * g.astype(jnp.float32)).astype(x.dtype)

def modulate(h, shift, scale):
    return h * (1 + scale) + shift

def squared_relu_mlp(h, w_in, w_out):
    return jnp.square(jax.nn.relu(h @ w_in)) @ w_out

def depthwise_conv3(u, w):
    return lax.conv_general_dilated(u, w.astype(u.dtype)[:, None, :], window_strides=(1,),
                                    padding=((1, 1),), dimension_numbers=('NWC', 'WIO', 'NWC'),
                                    feature_group_count=u.shape[-1])

def short_gated_conv(h, w_in, conv_w, w_out):
    b_gate, c_gate, v = jnp.split(h @ w_in, 3, axis=-1)
    return (b_gate * depthwise_conv3(c_gate * v, conv_w)) @ w_out

def gla_chunked(q, k, v, log_f, s0):
    bsz, seq, nh, dk = q.shape
    dv = v.shape[-1]
    nc = seq // HG_CHUNK

    def chunks(t):
        return t.reshape(bsz, nc, HG_CHUNK, nh, t.shape[-1]).transpose(1, 0, 3, 2, 4)

    qc, kc, vc = chunks(q.astype(jnp.float32)), chunks(k.astype(jnp.float32)), chunks(v)
    b = jnp.cumsum(chunks(log_f.astype(jnp.float32)), axis=3)
    b_mid = b[:, :, :, HG_CHUNK // 2 - 1:HG_CHUNK // 2]
    b_last = b[:, :, :, -1:]
    scores = jnp.einsum('nbhtk,nbhsk->nbhts', qc * jnp.exp(b - b_mid), kc * jnp.exp(b_mid - b))
    prefix = jnp.tril(jnp.ones((HG_CHUNK, HG_CHUNK), dtype=bool))
    o_intra = jnp.einsum('nbhts,nbhsv->nbhtv', jnp.where(prefix, scores, 0.0), vc)
    q_out = qc * jnp.exp(b)
    k_state = kc * jnp.exp(b_last - b)
    decay_chunk = jnp.exp(b_last[:, :, :, 0, :])

    def step(s, xs):
        q_o, k_s, v_s, a = xs
        o = jnp.einsum('bhtk,bhkv->bhtv', q_o, s)
        s = a[..., None] * s + jnp.einsum('bhtk,bhtv->bhkv', k_s, v_s)
        return s, o

    s_fin, o_inter = lax.scan(step, s0, (q_out, k_state, vc, decay_chunk))
    o = (o_intra + o_inter).transpose(1, 0, 3, 2, 4).reshape(bsz, seq, nh, dv)
    return o, s_fin

def hgrn2_mixer(h_ctx, h_lat, w_in, lower_bound, g_norm, w_out, ctx_out):
    bsz = h_lat.shape[0]
    s0 = jnp.zeros((bsz, HG_HEADS, HG_HEAD_DIM, HG_HEAD_DIM), jnp.float32)

    def heads(t):
        return t.reshape(*t.shape[:2], HG_HEADS, HG_HEAD_DIM)

    def forget(t):
        f = lower_bound + (1 - lower_bound) * jax.nn.sigmoid(t.astype(jnp.float32))
        return heads(1 - f), heads(jnp.log(f))

    def project(h):
        q, inp, gate, f_fwd, f_bwd = jnp.split(h @ w_in, 5, axis=-1)
        return heads(q), heads(inp), gate, forget(f_fwd), forget(f_bwd)

    def flip(t):
        return t[:, ::-1]

    qc, vc, gc, (kcf, lcf), (kcb, lcb) = project(h_ctx)
    ql, vl, gl, (klf, llf), (klb, llb) = project(h_lat)
    oc_f, st_f = gla_chunked(qc, kcf, vc, lcf, s0)
    ol_f, _ = gla_chunked(ql, klf, vl, llf, st_f)
    oc_b, st_b = gla_chunked(flip(qc), flip(kcb), flip(vc), flip(lcb), s0)
    ol_b, _ = gla_chunked(flip(ql), flip(klb), flip(vl), flip(llb), st_b)

    def readout(o, gate):
        o = rmsnorm(o, g_norm.reshape(HG_HEADS, HG_HEAD_DIM))
        o = o.reshape(*o.shape[:2], D_MODEL).astype(gate.dtype)
        return (o * jax.nn.silu(gate)) @ w_out

    y_lat = readout(ol_f + flip(ol_b), gl)
    y_ctx = readout(oc_f + flip(oc_b), gc) if ctx_out else None
    return y_ctx, y_lat

def s5_discretise(lam_re, lam_im, log_dt, b_re, b_im):
    lam_re = jnp.minimum(lam_re.astype(jnp.float32), -1e-4)
    lam_im = lam_im.astype(jnp.float32)
    dt = jnp.exp(log_dt.astype(jnp.float32))[:, None]
    mag = jnp.exp(lam_re * dt)
    a_re, a_im = mag * jnp.cos(lam_im * dt), mag * jnp.sin(lam_im * dt)
    den = lam_re * lam_re + lam_im * lam_im
    f_re = ((a_re - 1) * lam_re + a_im * lam_im) / den
    f_im = (a_im * lam_re - (a_re - 1) * lam_im) / den
    b_re, b_im = b_re.astype(jnp.float32), b_im.astype(jnp.float32)
    bb_re = f_re[..., None] * b_re - f_im[..., None] * b_im
    bb_im = f_re[..., None] * b_im + f_im[..., None] * b_re
    return a_re, a_im, bb_re, bb_im

def s5_scan(bu_re, bu_im, a_re, a_im, init, reverse):
    if init is not None:
        i_re, i_im = init
        first = -1 if reverse else 0
        bu_re = bu_re.at[:, first].add(a_re * i_re - a_im * i_im)
        bu_im = bu_im.at[:, first].add(a_re * i_im + a_im * i_re)
    seq = bu_re.shape[1]
    a_seq_re = jnp.broadcast_to(a_re, (1, seq) + a_re.shape)
    a_seq_im = jnp.broadcast_to(a_im, (1, seq) + a_im.shape)

    def combine(e1, e2):
        a1r, a1i, b1r, b1i = e1
        a2r, a2i, b2r, b2i = e2
        return (a2r * a1r - a2i * a1i, a2r * a1i + a2i * a1r,
                a2r * b1r - a2i * b1i + b2r, a2r * b1i + a2i * b1r + b2i)

    _, _, x_re, x_im = lax.associative_scan(combine, (a_seq_re, a_seq_im, bu_re, bu_im),
                                            axis=1, reverse=reverse)
    return x_re, x_im

def s5_mixer(h_ctx, h_lat, lam_re, lam_im, log_dt, b_re, b_im, c_re, c_im, d_skip, w_glu, ctx_out):
    def grouped(h):
        return h.reshape(*h.shape[:2], S5_GROUPS, S5_GROUP).astype(jnp.float32)

    u_c, u_l = grouped(h_ctx), grouped(h_lat)
    d = d_skip.reshape(S5_GROUPS, S5_GROUP).astype(jnp.float32)
    y_c, y_l = d * u_c, d * u_l
    for direction in range(2):
        reverse = direction == 1
        a_re, a_im, bb_re, bb_im = s5_discretise(lam_re[direction], lam_im[direction],
                                                 log_dt[direction], b_re, b_im)
        cr, ci = c_re[direction].astype(jnp.float32), c_im[direction].astype(jnp.float32)

        def drive(u):
            return (jnp.einsum('bsgc,gnc->bsgn', u, bb_re), jnp.einsum('bsgc,gnc->bsgn', u, bb_im))

        def readout(xr, xi):
            return jnp.einsum('bsgn,gcn->bsgc', xr, cr) - jnp.einsum('bsgn,gcn->bsgc', xi, ci)

        xc_re, xc_im = s5_scan(*drive(u_c), a_re, a_im, None, reverse)
        end = 0 if reverse else -1
        xl_re, xl_im = s5_scan(*drive(u_l), a_re, a_im, (xc_re[:, end], xc_im[:, end]), reverse)
        y_l = y_l + readout(xl_re, xl_im)
        if ctx_out:
            y_c = y_c + readout(xc_re, xc_im)

    def glu(y):
        z = jax.nn.gelu(y.reshape(*y.shape[:2], D_MODEL)).astype(w_glu.dtype)
        val, gate = jnp.split(z @ w_glu, 2, axis=-1)
        return val * jax.nn.sigmoid(gate)

    return (glu(y_c) if ctx_out else None), glu(y_l)

def neighbourhood_attention(h_ctx, h_lat, w_qkv, rpb, w_out, ctx_out):
    bsz, seq, _ = h_lat.shape
    rows = seq // GRID_W
    kr = min(NA_ROWS, rows)
    n_cb = GRID_W // NA_COLS
    n_loc = kr * NA_STRIP
    scale = NA_HEAD_DIM ** -0.5

    def heads(t):
        return t.reshape(*t.shape[:2], NA_HEADS, NA_HEAD_DIM)

    q_l, k_l, v_l = (heads(t) for t in jnp.split(h_lat @ w_qkv, 3, axis=-1))
    k_c, v_c = (heads(t) for t in jnp.split(h_ctx @ w_qkv[:, D_MODEL:], 2, axis=-1))

    r = jnp.arange(rows)
    key_rows = jnp.clip(r - kr // 2, 0, rows - kr)[:, None] + jnp.arange(kr)
    qcol = (jnp.arange(n_cb) * NA_COLS)[:, None] + jnp.arange(NA_COLS)
    key_cols = (jnp.clip(jnp.arange(n_cb) * NA_COLS - NA_COLS // 2, 0, GRID_W - NA_STRIP)[:, None]
                + jnp.arange(NA_STRIP))
    q_start = jnp.clip(qcol - NA_COLS // 2, 0, GRID_W - NA_COLS)[..., None]
    kcol = key_cols[:, None, :]
    in_win = jnp.tile((kcol >= q_start) & (kcol < q_start + NA_COLS), (1, 1, kr))
    dr = key_rows - r[:, None] + (NA_ROWS - 1)
    dc = jnp.clip(kcol - qcol[..., None], 1 - NA_COLS, NA_COLS - 1) + (NA_COLS - 1)
    bias = rpb[:, dr[:, None, None, :, None], dc[None, :, :, None, :]]
    bias = bias.reshape(NA_HEADS, rows, n_cb, NA_COLS, n_loc).astype(jnp.float32)

    def gather(t):
        g = t.reshape(bsz, rows, GRID_W, NA_HEADS, NA_HEAD_DIM)
        g = g[:, key_rows[:, None, :, None], key_cols[None, :, None, :]]
        return g.reshape(bsz, rows, n_cb, n_loc, NA_HEADS, NA_HEAD_DIM)

    q_b = q_l.reshape(bsz, rows, n_cb, NA_COLS, NA_HEADS, NA_HEAD_DIM)
    k_win, v_win = gather(k_l), gather(v_l)
    s_loc = jnp.einsum('brjqhd,brjkhd->bhrjqk', q_b, k_win).astype(jnp.float32) * scale + bias
    s_loc = jnp.where(in_win, s_loc, -jnp.inf)
    s_ctx = jnp.einsum('brjqhd,bkhd->bhrjqk', q_b, k_c).astype(jnp.float32) * scale
    p = jax.nn.softmax(jnp.concatenate([s_loc, s_ctx], axis=-1), axis=-1).astype(v_l.dtype)
    o = (jnp.einsum('bhrjqk,brjkhd->brjqhd', p[..., :n_loc], v_win)
         + jnp.einsum('bhrjqk,bkhd->brjqhd', p[..., n_loc:], v_c))
    y_lat = o.reshape(bsz, seq, D_MODEL) @ w_out
    y_ctx = None
    if ctx_out:
        q_c = heads(h_ctx @ w_qkv[:, :D_MODEL])
        s_cc = jnp.einsum('bqhd,bkhd->bhqk', q_c, k_c).astype(jnp.float32) * scale
        p_cc = jax.nn.softmax(s_cc, axis=-1).astype(v_c.dtype)
        o_c = jnp.einsum('bhqk,bkhd->bqhd', p_cc, v_c)
        y_ctx = o_c.reshape(bsz, h_ctx.shape[1], D_MODEL) @ w_out
    return y_ctx, y_lat

def first_inputs(seed: int = 0) -> dict:
    key = jax.random.key(seed)
    keys = iter(jax.random.split(key, 32))
    f32 = jnp.float32

    def normal(shape, std):
        return jax.random.normal(next(keys), shape, f32) * std

    n_a, n_b, n_c, n_d = (_layers_of(m) for m in range(N_MIXERS))
    d = D_MODEL
    lam_shape = (n_c, 2, S5_GROUPS, S5_STATE)
    return {
        'x': normal((BATCH, SEQ, d), 1.0),
        'c': normal((BATCH, d), 1.0),
        'ctx': normal((BATCH, CTX_LEN, d), 1.0),
        'c_ctx': normal((d,), 1.0),
        'ada_w': normal((DEPTH, d, N_MOD * d), 0.5 * d ** -0.5),
        'ada_b': normal((DEPTH, N_MOD * d), 0.02),
        'norm_gains': 1.0 + normal((DEPTH, 4, d), 0.02),
        'mlp_w_in': normal((DEPTH, d, D_FF), d ** -0.5),
        'mlp_w_out': normal((DEPTH, D_FF, d), D_FF ** -0.5),
        'sc_w_in': normal((n_a, d, 3 * d), d ** -0.5),
        'sc_conv': normal((n_a, CONV_W, d), CONV_W ** -0.5),
        'sc_w_out': normal((n_a, d, d), d ** -0.5),
        'hg_w_in': normal((n_b, d, 5 * d), d ** -0.5),
        'hg_lower_bound': normal((DEPTH, d), 0.1),
        'hg_norm': 1.0 + normal((n_b, d), 0.02),
        'hg_w_out': normal((n_b, d, d), d ** -0.5),
        's5_lam_re': -0.5 + normal(lam_shape, 0.01),
        's5_lam_im': math.pi * jnp.arange(S5_STATE, dtype=f32) + normal(lam_shape, 0.01),
        's5_log_dt': jax.random.uniform(next(keys), (n_c, 2, S5_GROUPS), f32,
                                        math.log(S5_DT_MIN), math.log(S5_DT_MAX)),
        's5_b_re': normal((n_c, S5_GROUPS, S5_STATE, S5_GROUP), (2 * S5_GROUP) ** -0.5),
        's5_b_im': normal((n_c, S5_GROUPS, S5_STATE, S5_GROUP), (2 * S5_GROUP) ** -0.5),
        's5_c_re': normal((n_c, 2, S5_GROUPS, S5_GROUP, S5_STATE), (2 * S5_STATE) ** -0.5),
        's5_c_im': normal((n_c, 2, S5_GROUPS, S5_GROUP, S5_STATE), (2 * S5_STATE) ** -0.5),
        's5_d': normal((n_c, d), 1.0),
        's5_w_glu': normal((n_c, d, 2 * d), d ** -0.5),
        'na_w_qkv': normal((n_d, d, 3 * d), d ** -0.5),
        'na_rpb': normal((n_d, NA_HEADS, 2 * NA_ROWS - 1, 2 * NA_COLS - 1), 0.1),
        'na_w_out': normal((n_d, d, d), d ** -0.5),
    }

def first_block(x, c, ctx, c_ctx, ada_w, ada_b, norm_gains, mlp_w_in, mlp_w_out,
              sc_w_in, sc_conv, sc_w_out, hg_w_in, hg_lower_bound, hg_norm, hg_w_out,
              s5_lam_re, s5_lam_im, s5_log_dt, s5_b_re, s5_b_im, s5_c_re, s5_c_im, s5_d, s5_w_glu,
              na_w_qkv, na_rpb, na_w_out):
    lb_all = jnp.cumsum(jax.nn.softmax(hg_lower_bound.astype(jnp.float32), axis=0), axis=0)
    lb_all = lb_all - lb_all[0]
    h_lat, h_ctx = x, ctx
    for i in range(DEPTH):
        kind, j = i % N_MIXERS, i // N_MIXERS
        ctx_out = i < DEPTH - 1
        mod_lat = [m[:, None, :] for m in jnp.split(jax.nn.silu(c) @ ada_w[i] + ada_b[i], N_MOD, axis=-1)]
        mod_ctx = jnp.split(jax.nn.silu(c_ctx) @ ada_w[i] + ada_b[i], N_MOD, axis=-1)
        g_pre, g_post, g_pre_ff, g_post_ff = norm_gains[i]
        a_lat = modulate(rmsnorm(h_lat, g_pre), mod_lat[0], mod_lat[1])
        a_ctx = modulate(rmsnorm(h_ctx, g_pre), mod_ctx[0], mod_ctx[1]) if (ctx_out or kind != 0) else None
        if kind == 0:
            y_lat = short_gated_conv(a_lat, sc_w_in[j], sc_conv[j], sc_w_out[j])
            y_ctx = short_gated_conv(a_ctx, sc_w_in[j], sc_conv[j], sc_w_out[j]) if ctx_out else None
        elif kind == 1:
            y_ctx, y_lat = hgrn2_mixer(a_ctx, a_lat, hg_w_in[j], lb_all[i], hg_norm[j], hg_w_out[j], ctx_out)
        elif kind == 2:
            y_ctx, y_lat = s5_mixer(a_ctx, a_lat, s5_lam_re[j], s5_lam_im[j], s5_log_dt[j], s5_b_re[j],
                                    s5_b_im[j], s5_c_re[j], s5_c_im[j], s5_d[j], s5_w_glu[j], ctx_out)
        else:
            y_ctx, y_lat = neighbourhood_attention(a_ctx, a_lat, na_w_qkv[j], na_rpb[j], na_w_out[j], ctx_out)
        h_lat = h_lat + mod_lat[2] * rmsnorm(y_lat.astype(h_lat.dtype), g_post)
        if ctx_out:
            h_ctx = h_ctx + mod_ctx[2] * rmsnorm(y_ctx.astype(h_ctx.dtype), g_post)
        f_lat = squared_relu_mlp(modulate(rmsnorm(h_lat, g_pre_ff), mod_lat[3], mod_lat[4]), mlp_w_in[i], mlp_w_out[i])
        h_lat = h_lat + mod_lat[5] * rmsnorm(f_lat.astype(h_lat.dtype), g_post_ff)
        if ctx_out:
            f_ctx = squared_relu_mlp(modulate(rmsnorm(h_ctx, g_pre_ff), mod_ctx[3], mod_ctx[4]), mlp_w_in[i], mlp_w_out[i])
            h_ctx = h_ctx + mod_ctx[5] * rmsnorm(f_ctx.astype(h_ctx.dtype), g_post_ff)
    return h_lat


DEPTH_2 = 2

N_ATTN_HEADS = 8
HEAD_DIM = D_MODEL // 16
ATTN_DIM = N_ATTN_HEADS * HEAD_DIM
Q_BLOCK = 128
FORGET_BIAS_MEAN = 3.0
POOL_WINDOWS = (2, 4, 8, 16)
N_POOL_GROUPS = len(POOL_WINDOWS)
POOL_GROUP_DIM = D_MODEL // 8
POOL_DIM = N_POOL_GROUPS * POOL_GROUP_DIM
EVEN_IN_DIM = 3 * ATTN_DIM + N_ATTN_HEADS + POOL_DIM
EVEN_MIX_DIM = ATTN_DIM + POOL_DIM
CONV_DIM = D_MODEL
CONV_WIDTH = 31
D_FF_2 = 2816
FFN_CONV_WIDTH = 3

N_EVEN = (DEPTH_2 + 1) // 2
N_ODD = DEPTH_2 // 2


def rms_norm(x, g):
    xf = x.astype(jnp.float32)
    y = xf * lax.rsqrt(jnp.mean(xf * xf, axis=-1, keepdims=True) + EPS)
    return (y * g.astype(jnp.float32)).astype(x.dtype)

def layer_norm(x, g, b):
    xf = x.astype(jnp.float32)
    mu = jnp.mean(xf, axis=-1, keepdims=True)
    xc = xf - mu
    y = xc * lax.rsqrt(jnp.mean(xc * xc, axis=-1, keepdims=True) + EPS)
    return (y * g.astype(jnp.float32) + b.astype(jnp.float32)).astype(x.dtype)

def causal_dwconv(x, w, b):
    k_width, ch = w.shape
    y = lax.conv_general_dilated(
        x, w[:, None, :].astype(x.dtype), window_strides=(1,), padding=[(k_width - 1, 0)],
        dimension_numbers=("NWC", "WIO", "NWC"), feature_group_count=ch)
    return y + b.astype(x.dtype)

def forgetting_attention(q, k, v, f_logit, q_g, k_g):
    bsz, seq, nh, dh = q.shape
    nb = seq // Q_BLOCK
    q = rms_norm(q, q_g)
    k = rms_norm(k, k_g)
    scale = 1.0 / math.sqrt(dh)
    c = jnp.cumsum(jax.nn.log_sigmoid(f_logit.astype(jnp.float32)), axis=1)
    c_k = jnp.transpose(c, (0, 2, 1))
    k_h = jnp.transpose(k, (0, 2, 1, 3))
    v_h = jnp.transpose(v, (0, 2, 1, 3))
    q_blocks = q.reshape(bsz, nb, Q_BLOCK, nh, dh).transpose(1, 0, 3, 2, 4)
    c_blocks = c.reshape(bsz, nb, Q_BLOCK, nh).transpose(1, 0, 3, 2)
    k_pos = jnp.arange(seq)

    def one_block(args):
        q_blk, cq_blk, blk = args
        q_pos = blk * Q_BLOCK + jnp.arange(Q_BLOCK)
        s = jnp.einsum("bhqd,bhkd->bhqk", q_blk, k_h).astype(jnp.float32) * scale
        s = s + cq_blk[..., :, None] - c_k[:, :, None, :]
        mask = k_pos[None, :] <= q_pos[:, None]
        s = jnp.where(mask[None, None], s, -jnp.inf)
        p = jax.nn.softmax(s, axis=-1)
        return jnp.einsum("bhqk,bhkd->bhqd", p.astype(v_h.dtype), v_h)

    out = lax.map(one_block, (q_blocks, c_blocks, jnp.arange(nb)))
    return out.transpose(1, 0, 3, 2, 4).reshape(bsz, seq, nh * dh)

def multiscale_pool(u, w_pool, pool_scale):
    bsz, seq, _ = u.shape
    ug = u.reshape(bsz, seq, N_POOL_GROUPS, POOL_GROUP_DIM)
    csz = jnp.pad(jnp.cumsum(ug.astype(jnp.float32), axis=1), ((0, 0), (1, 0), (0, 0), (0, 0)))
    pos = jnp.arange(1, seq + 1, dtype=jnp.float32)
    outs = []
    for g, w in enumerate(POOL_WINDOWS):
        upper = csz[:, 1:, g]
        lower = jnp.pad(csz[:, : seq + 1 - w, g], ((0, 0), (w - 1, 0), (0, 0)))
        count = jnp.minimum(pos, float(w))[None, :, None]
        outs.append((upper - lower) / count)
    pooled = jnp.stack(outs, axis=2).astype(u.dtype)
    mixed = pooled - ug
    y = jnp.einsum("bsgc,gcd->bsgd", mixed, w_pool).reshape(bsz, seq, POOL_DIM)
    return y * pool_scale

def even_mixer(h, w_in, b_f, q_g, k_g, w_pool, pool_scale, w_out):
    bsz, seq, _ = h.shape
    z = h @ w_in
    o = 0
    q = z[..., o:o + ATTN_DIM].reshape(bsz, seq, N_ATTN_HEADS, HEAD_DIM); o += ATTN_DIM
    k = z[..., o:o + ATTN_DIM].reshape(bsz, seq, N_ATTN_HEADS, HEAD_DIM); o += ATTN_DIM
    v = z[..., o:o + ATTN_DIM].reshape(bsz, seq, N_ATTN_HEADS, HEAD_DIM); o += ATTN_DIM
    f_logit = z[..., o:o + N_ATTN_HEADS] + b_f; o += N_ATTN_HEADS
    u = z[..., o:o + POOL_DIM]
    a_out = forgetting_attention(q, k, v, f_logit, q_g, k_g)
    p_out = multiscale_pool(u, w_pool, pool_scale)
    return jnp.concatenate([a_out, p_out], axis=-1) @ w_out

def conformer_conv(h, w_pw1, dw_w, dw_b, ln_g, ln_b, w_pw2):
    a, g = jnp.split(h @ w_pw1, 2, axis=-1)
    u = a * jax.nn.sigmoid(g)
    u = causal_dwconv(u, dw_w, dw_b)
    u = jax.nn.silu(layer_norm(u, ln_g, ln_b))
    return u @ w_pw2

def conv_ffn(h, w_up, conv_w, conv_b, w_down):
    u = causal_dwconv(h @ w_up, conv_w, conv_b)
    gate, val = jnp.split(u, 2, axis=-1)
    return (jax.nn.silu(gate) * val) @ w_down

def second_inputs(seed: int = 0) -> dict:
    key = jax.random.key(seed)
    ks = jax.random.split(key, 24)
    nrm = lambda k, shape, s: jax.random.normal(k, shape, jnp.float32) * s
    d = D_MODEL
    return {
        "x": nrm(ks[0], (BATCH, SEQ, d), 1.0),
        "even_norm_g": 1.0 + nrm(ks[1], (N_EVEN, d), 0.05),
        "even_w_in": nrm(ks[2], (N_EVEN, d, EVEN_IN_DIM), d ** -0.5),
        "even_b_f": FORGET_BIAS_MEAN + nrm(ks[3], (N_EVEN, N_ATTN_HEADS), 0.5),
        "even_q_norm_g": 1.0 + nrm(ks[4], (N_EVEN, HEAD_DIM), 0.05),
        "even_k_norm_g": 1.0 + nrm(ks[5], (N_EVEN, HEAD_DIM), 0.05),
        "even_w_pool": nrm(ks[6], (N_EVEN, N_POOL_GROUPS, POOL_GROUP_DIM, POOL_GROUP_DIM), POOL_GROUP_DIM ** -0.5),
        "even_pool_scale": 1.0 + nrm(ks[7], (N_EVEN, POOL_DIM), 0.1),
        "even_w_out": nrm(ks[8], (N_EVEN, EVEN_MIX_DIM, d), EVEN_MIX_DIM ** -0.5),
        "odd_norm_g": 1.0 + nrm(ks[9], (N_ODD, d), 0.05),
        "odd_w_pw1": nrm(ks[10], (N_ODD, d, 2 * CONV_DIM), d ** -0.5),
        "odd_dw_w": nrm(ks[11], (N_ODD, CONV_WIDTH, CONV_DIM), CONV_WIDTH ** -0.5),
        "odd_dw_b": nrm(ks[12], (N_ODD, CONV_DIM), 0.02),
        "odd_ln_g": 1.0 + nrm(ks[13], (N_ODD, CONV_DIM), 0.05),
        "odd_ln_b": nrm(ks[14], (N_ODD, CONV_DIM), 0.02),
        "odd_w_pw2": nrm(ks[15], (N_ODD, CONV_DIM, d), CONV_DIM ** -0.5),
        "ffn_norm_g": 1.0 + nrm(ks[16], (DEPTH_2, d), 0.05),
        "ffn_w_up": nrm(ks[17], (DEPTH_2, d, 2 * D_FF_2), d ** -0.5),
        "ffn_conv_w": nrm(ks[18], (DEPTH_2, FFN_CONV_WIDTH, 2 * D_FF_2), FFN_CONV_WIDTH ** -0.5),
        "ffn_conv_b": nrm(ks[19], (DEPTH_2, 2 * D_FF_2), 0.02),
        "ffn_w_down": nrm(ks[20], (DEPTH_2, D_FF_2, d), D_FF_2 ** -0.5),
    }

def second_block(x, even_norm_g, even_w_in, even_b_f, even_q_norm_g, even_k_norm_g, even_w_pool,
              even_pool_scale, even_w_out, odd_norm_g, odd_w_pw1, odd_dw_w, odd_dw_b, odd_ln_g,
              odd_ln_b, odd_w_pw2, ffn_norm_g, ffn_w_up, ffn_conv_w, ffn_conv_b, ffn_w_down):
    for layer in range(DEPTH_2):
        i = layer // 2
        if layer % 2 == 0:
            h = rms_norm(x, even_norm_g[i])
            x = x + even_mixer(h, even_w_in[i], even_b_f[i], even_q_norm_g[i], even_k_norm_g[i],
                               even_w_pool[i], even_pool_scale[i], even_w_out[i])
        else:
            h = rms_norm(x, odd_norm_g[i])
            x = x + conformer_conv(h, odd_w_pw1[i], odd_dw_w[i], odd_dw_b[i], odd_ln_g[i],
                                   odd_ln_b[i], odd_w_pw2[i])
        h = rms_norm(x, ffn_norm_g[layer])
        x = x + conv_ffn(h, ffn_w_up[layer], ffn_conv_w[layer], ffn_conv_b[layer], ffn_w_down[layer])
    return x


def setup_inputs(seed=0):
    out = dict(first_inputs(seed))
    for name, value in second_inputs(seed + 1).items():
        if name != "x":
            out[name + "_2"] = value
    return out


def reference(
    x, c, ctx, c_ctx, ada_w, ada_b, norm_gains, mlp_w_in, mlp_w_out, sc_w_in, sc_conv, sc_w_out,
    hg_w_in, hg_lower_bound, hg_norm, hg_w_out, s5_lam_re, s5_lam_im, s5_log_dt, s5_b_re,
    s5_b_im, s5_c_re, s5_c_im, s5_d, s5_w_glu, na_w_qkv, na_rpb, na_w_out, even_norm_g_2,
    even_w_in_2, even_b_f_2, even_q_norm_g_2, even_k_norm_g_2, even_w_pool_2, even_pool_scale_2,
    even_w_out_2, odd_norm_g_2, odd_w_pw1_2, odd_dw_w_2, odd_dw_b_2, odd_ln_g_2, odd_ln_b_2,
    odd_w_pw2_2, ffn_norm_g_2, ffn_w_up_2, ffn_conv_w_2, ffn_conv_b_2, ffn_w_down_2,
):
    x = first_block(
        x, c, ctx, c_ctx, ada_w, ada_b, norm_gains, mlp_w_in, mlp_w_out, sc_w_in, sc_conv,
        sc_w_out, hg_w_in, hg_lower_bound, hg_norm, hg_w_out, s5_lam_re, s5_lam_im, s5_log_dt,
        s5_b_re, s5_b_im, s5_c_re, s5_c_im, s5_d, s5_w_glu, na_w_qkv, na_rpb, na_w_out,
    )
    return second_block(
        x, even_norm_g_2, even_w_in_2, even_b_f_2, even_q_norm_g_2, even_k_norm_g_2,
        even_w_pool_2, even_pool_scale_2, even_w_out_2, odd_norm_g_2, odd_w_pw1_2, odd_dw_w_2,
        odd_dw_b_2, odd_ln_g_2, odd_ln_b_2, odd_w_pw2_2, ffn_norm_g_2, ffn_w_up_2, ffn_conv_w_2,
        ffn_conv_b_2, ffn_w_down_2,
    )


_drawn_inputs = setup_inputs


def setup_inputs(seed=0):
    import zlib

    import numpy as np

    out = dict(_drawn_inputs(seed))
    spreads = {}
    factors = {'norm_gains': 3.136,
     'even_q_norm_g_2': 6.268,
     'even_k_norm_g_2': 4.957,
     'odd_dw_b_2': 3.386,
     'odd_ln_b_2': 6.951,
     'ffn_conv_b_2': 3.341,
     'odd_norm_g_2': 3.405,
     'odd_ln_g_2': 3.218}
    for name, (base, spread) in spreads.items():
        noise = np.random.default_rng([zlib.crc32(name.encode()), seed]).standard_normal(out[name].shape)
        drawn = base * np.exp(spread * noise) if base else spread * noise
        out[name] = jnp.asarray(drawn.astype(out[name].dtype))
    for name, factor in factors.items():
        out[name] = (out[name] * factor).astype(out[name].dtype)
    return out
```

```python
from contextlib import ExitStack

import concourse.bass as bass
from concourse import mybir

F32 = mybir.dt.float32
F32R = mybir.dt.float32r
ALU = mybir.AluOpType
ACT = mybir.ActivationFunctionType
AX = mybir.AxisListType
ds = bass.ds

P = 128
T = 512
TB = T // P
D = 1024
DC = D // P
F1 = 4 * D
F2 = 2816
NG = F2 // P
HEADS, DH = 8, 64
WINDOWS = (2, 4, 8, 16)
WINDOW_STEPS = sum(w.bit_length() - 1 + w - 1 for w in WINDOWS)
TAPS = 31
PADU = TAPS - 1
EPS = 1e-6
UW = 256
MASKED = -1e30

U_SCIN, U_SCOUT, U_MLP = 0, 12, 16
U_EVEN = U_MLP + 32
U_EOUT = U_EVEN + 8
U_PW1 = U_EOUT + 4 + 34
U_PW2 = U_PW1 + 8
U_FFN = (U_EOUT + 4, U_PW2 + 4)
U_END = U_FFN[1] + 34
GROUPS = ((0, 4, 8), (4, 4, 8), (8, 3, 6))

ROWS, TILE_ROWS = {}, []
for _names in ([("ada_b", 48), ("gains", 32), ("sc_conv", 24), ("c", 8)],
               [("even_norm", 8), ("odd_norm", 8), ("dw_b", 8), ("ln_g", 8), ("ln_b", 8),
                ("ffn_norm", 16), ("pool_scale", 4), ("q_g", 1), ("k_g", 1)],
               [("dw_w0", 124)], [("dw_w1", 124)],
               [("fw00", 44), ("fw01", 44)], [("fw02", 44), ("fb0", 44)],
               [("fw10", 44), ("fw11", 44)], [("fw12", 44), ("fb1", 44)]):
    _row = 0
    for _name, _n in _names:
        ROWS[_name] = (len(TILE_ROWS), _row)
        _row += _n
    TILE_ROWS.append(_row)
VT = len(TILE_ROWS)
TILE_COL = [sum(TILE_ROWS[:t]) for t in range(VT)]
S_EPS, S_BF, S_CS, S_MOD, S_DUMP = 0, 1, 2, 10, 58
S_MX, S_NM, S_RS, S_RR = 112, 120, 128, 136
S_GS0, S_MG0, S_GS1, S_MG1, S_Q8 = 66, 74, 82, 90, 98

ST_X0, ST_Y0, ST_X1, ST_Y1, ST_X2, ST_F0, ST_X3, ST_MEAN, ST_VAR, ST_F1 = range(10)


def squares(stat):
    return stat if stat <= ST_MEAN else stat - 1


def program(nc, i, out):
    ctx = ExitStack()
    with ctx:
        base = (nc.sbuf_base + 63) // 64 * 64

        def at(name, kib, shape, dt=F32):
            return nc.alloc_sbuf_tensor_at(name, shape, dt, offset=base + int(kib * 1024))

        def sem(name):
            return ctx.enter_context(nc.semaphore(name))

        X = at("X", 0, [P, DC, T])
        XH = at("XH", 16, [P, DC, T], F32R)
        XL = at("XL", 32, [P, DC, T], F32R)
        OT = at("OT", 16, [P, TB, T])
        PS = at("PS", 24, [P, 4, T])
        HH = at("HH", 48, [P, 8, T], F32R)
        HL = at("HL", 64, [P, 8, T], F32R)
        VROW = at("VROW", 48, [P, VT, P])
        CR = at("CR", 48, [97, HEADS, T])
        UP = at("UP", 64, [P, 4, 16 + T])
        PA = at("PA", 72.5, [P, 2, 16 + T])
        RAW = at("RAW", 80, [P, 2, 8, UW])
        WH = at("WH", 96, [P, 2, 8, UW], F32R)
        WL = at("WL", 112, [P, 2, 8, UW], F32R)
        Y = at("Y", 128, [P, DC, T])
        XROW = at("XROW", 128, [P, TB, D])
        QK = at("QK", 128, [P, 8, T])
        UPAD = at("UPAD", 128, [P, DC, PADU + T])
        VCOL = at("VCOL", 145, [P, sum(TILE_ROWS)])
        MACC = at("MACC", 148.5, [P, 6 * D])
        SQT = at("SQT", 148.5, [P, 8, T])
        V = at("V", 164.5, [P, TB, T])
        CV = at("CV", 148.5, [P, DC, T])
        ARAW = at("ARAW", 172.5, [P, 2, 8, UW])
        FRAW = at("FRAW", 172.5, [P, 8, P])
        FH = at("FH", 176.5, [P, 8, P], F32R)
        FL = at("FL", 180.5, [P, 8, P], F32R)
        WP = at("WP", 184.5, [P, 4, P])
        QS = at("QS", 172.5, [97, 2, T])
        KS = at("KS", 176.5, [97, 2, T])
        PR = at("PR", 180.5, [P, 2, T])
        PT = at("PT", 186.5, [P, T])
        TA = at("TA", 188.5, [P, 2, T])
        TF = at("TF", 192.5, [P, 2, T])
        CA = at("CA", 188.5, [8, 2, 256 + T])
        ZP = at("ZP", 196.5, [P, 2, 2 + T])
        R = at("R", 200.75, [P, T])
        SQ = at("SQ", 202.75, [P, T])
        IDENT = at("IDENT", 204.75, [P, P])
        ONES = at("ONES", 205.25, [P, P])
        BD = at("BD", 205.75, [P, P])
        MASK = at("MASK", 206.25, [P, P])
        small = at("small", 206.75, [P, 144])
        PS_ = ctx.enter_context(nc.psum_tensor("PSUM", [P, 8, T], F32))
        ST_BANK, COL_BANK = 4, 5

        def col(name, k=0, n=1):
            t, r = ROWS[name]
            return VCOL[:, ds(k + (TILE_COL[t] + r), n)] if not isinstance(k, int) else \
                VCOL[:, TILE_COL[t] + r + k:TILE_COL[t] + r + k + n]

        def sc_(k, n=1):
            return small[:, k:k + n]

        s_raw = [sem("unit_loaded_even"), sem("unit_loaded_odd")]
        s_hi, s_lo = sem("half_unit_hi"), sem("half_unit_lo")
        s_mm, s_ev = sem("unit_multiplied"), sem("unit_banks_emptied")
        s_x, s_h = sem("input_chunk_ready"), sem("hidden_chunk_ready")
        s_xin = sem("x_rows_loaded")
        s_vin, s_vin2 = sem("vectors_loaded"), sem("bf_loaded")
        s_const, s_const0 = sem("constants_ready"), sem("constants_cleared")
        s_xt, s_xe, s_vt, s_ve = sem("x_turned"), sem("x_copied"), sem("vectors_turned"), sem("vectors_copied")
        s_cs, s_sm = sem("silu_c"), sem("small_vector_step")
        s_ar = [sem("mod_weights_even"), sem("mod_weights_odd")]
        s_ad, s_as = sem("mod_unit_summed"), sem("mod_step")
        s_ac = sem("mod_columns")
        s_xu, s_sqr, s_sqa = sem("chunk_to_square"), sem("chunk_squared"), sem("square_sum_step")
        s_ss, s_ln, s_r = sem("channel_sum"), sem("ln_of_sum"), sem("rms_ready")
        sp_t, sp_y, sp_h = sem("split_scaled"), sem("split_shifted"), sem("split_hi")
        s_pn = sem("postnorm_scaled")
        c_z, c_t, c_y, c_g, c_h = (sem("gconv_" + x) for x in ("cv", "centre", "taps", "gated", "hi"))
        m_r, m_f, m_h = (sem("mlp_" + x) for x in ("relu", "squared", "hi"))
        f_z, f_t, f_y, f_s, f_p, f_h = (sem("ffn_" + x) for x in ("z", "centre", "taps", "silu", "product", "hi"))
        s_fw, s_fh, s_fl, s_f = sem("forget_w"), sem("forget_w_hi"), sem("forget_w_lo"), sem("forget_logits")
        e_f, e_a, e_c, e_cr = sem("logit_biased"), sem("logit_act"), sem("cumsum_step"), sem("decay_rows")
        e_q, e_sq, s_hn, e_ln, e_r = (sem("qk_" + x) for x in ("chunk", "squared", "head_sum", "ln", "rms"))
        e_u, e_w = sem("pool_input"), sem("window_step")
        s_wp, e_mx, s_pm, e_ph = sem("pool_w"), sem("pool_mixed"), sem("pool_product"), sem("pool_hi")
        a_qk, a_row = sem("head_qk"), sem("head_decay_rows")
        a_s, a_mask, a_max, a_neg, a_e, a_rr = (sem("attn_" + x) for x in ("scores", "mask", "max", "neg", "exp", "recip"))
        a_t, a_tc, a_o, a_oe = (sem("attn_" + x) for x in ("turned", "copied", "out", "out_copied"))
        a_ot, a_h = sem("attn_out_turned"), sem("attn_out_hi")
        g_c, g_s, g_u, g_v = (sem("conf_" + x) for x in ("gate", "sigmoid", "input", "tap"))
        n_m, n_c, n_t, n_a, n_y, n_h = (sem("ln_" + x) for x in ("mean", "centred", "scaled", "silu", "y", "hi"))
        s_zero = sem("pads_cleared")
        s_yt, s_out = sem("out_turned"), sem("out_stored")
        s_yc = [sem("out_copied_left"), sem("out_copied_right")]

        block = ctx.enter_context(nc.Block())

        def wview(name, layer=0):
            return i[name][layer].rearrange("(k p) n -> p k n", p=P)

        @block.sync
        def _(sp):
            def load(u, j, w, c0, k0=0, kn=8):
                if not (isinstance(u, int) and u < 2):
                    sp.wait_ge(s_lo, u * 2 - 2)
                sp.dma_start(RAW[:, j, 0:kn, :], w[:, k0:k0 + kn, ds(c0, UW)]).then_inc(s_raw[j], 16)

            def load_mod(a):
                if a >= 2:
                    sp.wait_ge(s_ad, a - 1)
                sp.dma_start(ARAW[:, a % 2], ada[:, :, a * UW:a * UW + UW]).then_inc(s_ar[a % 2], 16)

            ada = wview("ada_w")
            x_rows = i["x"][0].rearrange("(b p) d -> p b d", p=P)
            def rows(name, ap, n):
                t, r = ROWS[name]
                sp.dma_start(VROW[r:r + n, t, :], ap).then_inc(s_vin, 16)

            def r128(ap):
                return ap.rearrange("(r p) -> r p", p=P)

            rows("c", r128(i["c"][0]), 8)
            rows("ada_b", r128(i["ada_b"][0]), 48)
            rows("gains", i["norm_gains"][0].rearrange("g (r p) -> (g r) p", p=P), 32)
            rows("sc_conv", i["sc_conv"][0].rearrange("g (r p) -> (g r) p", p=P), 24)
            load_mod(0)
            load_mod(1)
            sp.dma_start(XROW[:, :, :], x_rows).then_inc(s_xin, 16)
            rows("even_norm", r128(i["even_norm_g_2"][0]), 8)
            rows("odd_norm", r128(i["odd_norm_g_2"][0]), 8)
            rows("dw_b", r128(i["odd_dw_b_2"][0]), 8)
            rows("ln_g", r128(i["odd_ln_g_2"][0]), 8)
            rows("ln_b", r128(i["odd_ln_b_2"][0]), 8)
            rows("ffn_norm", i["ffn_norm_g_2"].rearrange("g (r p) -> (g r) p", p=P), 16)
            rows("pool_scale", r128(i["even_pool_scale_2"][0]), 4)
            for name in ("q", "k"):
                t, r = ROWS[name + "_g"]
                for half in range(2):
                    sp.dma_start(VROW[r:r + 1, t, half * DH:half * DH + DH], i[f"even_{name}_norm_g_2"]
                                 ).then_inc(s_vin, 16)
            dw = i["odd_dw_w_2"][0].rearrange("g (r p) -> (g r) p", p=P)
            rows("dw_w0", dw[0:124], 124)
            rows("dw_w1", dw[124:248], 124)
            for layer in range(2):
                for tap in range(3):
                    rows(f"fw{layer}{tap}", r128(i["ffn_conv_w_2"][layer, tap]), 2 * NG)
                rows(f"fb{layer}", r128(i["ffn_conv_b_2"][layer]), 2 * NG)
            sp.dma_start(small[0:8, S_BF:S_BF + 1], i["even_b_f_2"].rearrange("a h -> h a")).then_inc(s_vin2, 16)

            scin, scout = wview("sc_w_in"), wview("sc_w_out")
            order = (D, 2 * D, 0)
            load(0, 0, scin, order[0])
            load(1, 1, scin, order[1])
            for a in range(2, 10):
                load_mod(a)
            for u in range(2, 12):
                load(u, u % 2, scin, order[u % 3] + u // 3 * UW)
                load_mod(8 + u)
            for u in range(12, 16):
                load(u, u % 2, scout, (u - 12) * UW)
                load_mod(8 + u) if 8 + u < 24 else None
            w_in, w_out = wview("mlp_w_in"), wview("mlp_w_out")
            for g in range(4):
                with sp.Fori(0, 2) as it:
                    for j in range(2):
                        load(it * 2 + (U_MLP + 8 * g + j), j, w_in, it * (2 * UW) + (g * D + j * UW))
                with sp.Fori(0, 2) as it:
                    for j in range(2):
                        load(it * 2 + (U_MLP + 8 * g + 4 + j), j, w_out, it * (2 * UW) + j * UW, 8 * g)
            ein = wview("even_w_in_2")
            sp.wait_ge(s_ad, 24)
            sp.dma_start(FRAW[:, :, :], ein[:, :, 1536:1536 + P]).then_inc(s_fw, 16)
            sp.dma_start(WP[:, :, :], i["even_w_pool_2"][0].rearrange("g c d -> c g d")).then_inc(s_wp, 16)
            with sp.Fori(0, 3) as it:
                for j in range(2):
                    load(it * 2 + (U_EVEN + j), j, ein, it * (2 * UW) + j * UW)
            for j in range(2):
                load(U_EVEN + 6 + j, j, ein, 1544 + j * UW)
            eout = wview("even_w_out_2")
            load(U_EOUT, 0, eout, 0)
            load(U_EOUT + 1, 1, eout, UW)
            sp.wait_ge(e_c, 12)
            sp.dma_start(CR[64:65, :, :], CA[:, 1, 256:256 + T]).then_inc(e_cr, 16)
            sp.dma_start(CR[96:97, :, :], CA[:, 0, 256:256 + T]).then_inc(e_cr, 16)
            load(U_EOUT + 2, 0, eout, 2 * UW)
            load(U_EOUT + 3, 1, eout, 3 * UW)

            def feed_forward(layer):
                up, down = wview("ffn_w_up_2", layer), wview("ffn_w_down_2", layer)
                u = U_FFN[layer]
                for first, steps, kn in GROUPS:
                    with sp.Fori(0, steps) as it:
                        load(it * 2 + u, 0, up, it * UW + first * UW)
                        load(it * 2 + (u + 1), 1, up, it * UW + (F2 + first * UW))
                    u += 2 * steps
                    with sp.Fori(0, 2) as it:
                        for j in range(2):
                            load(it * 2 + (u + j), j, down, it * (2 * UW) + j * UW, 2 * first, kn)
                    u += 4

            feed_forward(0)
            pw1, pw2 = wview("odd_w_pw1_2"), wview("odd_w_pw2_2")
            with sp.Fori(0, 4) as it:
                load(it * 2 + U_PW1, 0, pw1, it * UW + D)
                load(it * 2 + (U_PW1 + 1), 1, pw1, it * P + it * P)
            with sp.Fori(0, 2) as it:
                for j in range(2):
                    load(it * 2 + (U_PW2 + j), j, pw2, it * (2 * UW) + j * UW)
            feed_forward(1)
            for b in range(TB):
                sp.wait_ge(s_yc[0], b + 1)
                sp.wait_ge(s_yc[1], b + 1)
                sp.dma_start(out[0, b * P:b * P + P, :], XROW[:, b, :]).then_inc(s_out, 16)
            sp.wait_ge(s_out, 16 * TB)

        @block.gpsimd
        def _(pool):
            for m, v in ((IDENT, 0.0), (ONES, 1.0), (BD, 0.0), (MASK, 0.0)):
                pool.memset(m[:, :], v).then_inc(s_const0, 1)
            pool.memset(sc_(S_EPS), EPS).then_inc(s_const, 1)
            pool.wait_ge(s_const0, 4)
            pool.affine_select(out=IDENT[:, :], in_=IDENT[:, :], compare_op=ALU.not_equal, fill=1.0, base=0,
                               pattern=[[-1, P]], channel_multiplier=1).then_inc(s_const, 1)
            pool.affine_select(out=MASK[:, :], in_=MASK[:, :], compare_op=ALU.is_ge, fill=MASKED, base=0,
                               pattern=[[-1, P]], channel_multiplier=1).then_inc(s_const, 1)
            for h in range(2):
                pool.wait_ge(s_const, 3 + h)
                pool.memset(BD[h * DH:h * DH + DH, h * DH:h * DH + DH], 1.0).then_inc(s_const, 1)
            pool.wait_ge(s_const, 5)
            pool.memset(ZP[:, :, 0:1], 0.0).then_inc(s_const, 1)
            pool.wait_ge(s_const, 6)
            pool.memset(ZP[:, :, T + 1:T + 2], 0.0).then_inc(s_const, 1)

            pool.wait_ge(s_mm, U_MLP + 32)
            pool.memset(UP[:, :, 0:16], 0.0).then_inc(s_zero, 1)
            pool.wait_ge(e_u, 4)
            pool.wait_ge(s_mm, U_EVEN + 8)
            step = 0
            for g, w in enumerate(WINDOWS):
                src, have = UP[:, g, :], 1
                while have < w:
                    last = 2 * have == w
                    lo = 16 if last else 2 * have - 1
                    dst = PS[:, g, :] if last else PA[:, step % 2, lo:]
                    if step:
                        pool.wait_ge(e_w, step)
                    pool.tensor_tensor(dst, src[:, lo:], src[:, lo - have:16 + T - have], ALU.add).then_inc(e_w, 1)
                    src, have, step = PA[:, step % 2, :], 2 * have, step + 1
            for g, w in enumerate(WINDOWS):
                for t in range(w - 1):
                    pool.wait_ge(e_w, step)
                    pool.tensor_scalar(PS[:, g, t:t + 1], PS[:, g, t:t + 1], float(w) / (t + 1), 0.0,
                                       ALU.mult, ALU.add).then_inc(e_w, 1)
                    step += 1

        @block.scalar
        def _(act):
            def hi_half(u, j, half, kn=8):
                if half == 0:
                    if not (isinstance(u, int) and u < 2):
                        act.wait_ge(s_mm, u - 1)
                    act.wait_ge(s_raw[j], (u - j) * 8 + 16)
                a, b = (0, 4) if half == 0 else (4, kn)
                act.activation(WH[:, j, a:b, :], RAW[:, j, a:b, :], ACT.Copy).then_inc(s_hi, 1)

            def square(stat, m, src):
                q = 8 * squares(stat) + m
                act.wait_ge(s_xu, q + 1)
                if m_at_least(m, 2):
                    act.wait_ge(s_sqa, m + (9 * stat))
                act.activation(TF[:, m % 2 if isinstance(m, int) else 0, :], src, ACT.Square).then_inc(s_sqr, 1)

            def m_at_least(m, n):
                return not isinstance(m, int) or m >= n

            def rms(stat, scale):
                act.wait_ge(s_ss, stat + 1)
                act.activation(R[:, :], PS_[:, ST_BANK, :], ACT.Ln, bias=sc_(S_EPS), scale=scale).then_inc(s_ln, 1)
                act.wait_ge(s_ln, stat + 1)
                act.activation(R[:, :], R[:, :], ACT.Exp, scale=-0.5).then_inc(s_r, 1)

            def split_shift(m, gs, sh):
                for c in range(DC):
                    act.wait_ge(sp_t, 8 * m + c + 1)
                    act.activation(TF[:, c % 2, :], TA[:, c % 2, :], ACT.Identity, scale=sc_(gs + c),
                                   bias=sc_(sh + c)).then_inc(sp_y, 1)
                    act.wait_ge(sp_y, 8 * m + c + 1)
                    act.activation(XH[:, c, :], TF[:, c % 2, :], ACT.Copy).then_inc(sp_h, 1)

            def split(m, gain, k):
                for c in range(DC):
                    act.wait_ge(sp_t, 8 * m + c + 1)
                    act.activation(XH[:, c, :], TA[:, c % 2, :], ACT.Copy, scale=col(gain, k + c)).then_inc(sp_h, 1)

            def out_window(u, stat, n0, nxt=8, prep=True):
                j = 0 if prep is None else None

            act.wait_ge(s_ve, 1)
            act.activation(sc_(S_CS, 8), col("c", 0, 8), ACT.Silu).then_inc(s_cs, 1)
            for c in range(DC):
                square(ST_X0, c, X[:, c, :])
            act.wait_ge(s_const, 1)
            rms(ST_X0, 1.0 / D)
            for u in range(2):
                hi_half(u, u, 0)
                hi_half(u, u, 1)
            act.wait_ge(s_sm, 3)
            split_shift(0, S_GS0, S_MOD)

            for u in range(12):
                hi_half(u + 2, u % 2, 0)
                step = u // 3
                if u % 3 == 1:
                    for c in range(2):
                        n = 2 * step + c
                        act.wait_ge(c_z, n + 1)
                        act.activation(TA[:, c, :], ZP[:, c, 1:T + 1], ACT.Copy, scale=col("sc_conv", 8 + n)
                                       ).then_inc(c_t, 1)
                hi_half(u + 2, u % 2, 1)
                if u % 3 == 2:
                    for c in range(2):
                        n = 2 * step + c
                        act.wait_ge(c_g, n + 1)
                        act.activation(HH[:, n, :], TA[:, c, :], ACT.Copy).then_inc(c_h, 1)
            for u in range(12, 16):
                hi_half(u + 2, u % 2, 0)
                hi_half(u + 2, u % 2, 1)
                for c in range(2):
                    n = 2 * (u - 12) + c
                    square(ST_Y0, n, Y[:, n, :])
            rms(ST_Y0, 1.0 / D)
            for c in range(DC):
                square(ST_X1, c, X[:, c, :])
            rms(ST_X1, 1.0 / D)
            split_shift(1, S_GS1, S_MOD + 24)

            for g in range(4):
                with act.Fori(0, 2) as it:
                    for j in range(2):
                        u = it * 2 + (U_MLP + 8 * g + j)
                        hi_half(u + 2, j, 0)
                        for c in range(2):
                            act.wait_ge(m_r, it * 4 + (8 * g + 2 * j + c + 1))
                            act.activation(TF[:, c, :], TA[:, c, :], ACT.Square).then_inc(m_f, 1)
                        hi_half(u + 2, j, 1)
                        for c in range(2):
                            act.wait_ge(m_f, it * 4 + (8 * g + 2 * j + c + 1))
                            act.activation(HH[:, ds(it * 4 + (2 * j + c), 1), :], TF[:, c:c + 1, :], ACT.Copy
                                           ).then_inc(m_h, 1)
                if g < 3:
                    with act.Fori(0, 2) as it:
                        for j in range(2):
                            u = it * 2 + (U_MLP + 8 * g + 4 + j)
                            hi_half(u + 2, j, 0)
                            hi_half(u + 2, j, 1)
            for u in range(U_MLP + 28, U_MLP + 32):
                hi_half(u + 2, u % 2, 0)
                hi_half(u + 2, u % 2, 1)
                for c in range(2):
                    n = 2 * (u - U_MLP - 28) + c
                    square(ST_Y1, n, Y[:, n, :])
            rms(ST_Y1, 1.0 / D)
            for c in range(DC):
                square(ST_X2, c, X[:, c, :])
            rms(ST_X2, 1.0 / D)
            act.wait_ge(s_fw, 16)
            act.activation(FH[:, :, :], FRAW[:, :, :], ACT.Copy).then_inc(s_fh, 1)
            split(2, "even_norm", 0)

            act.wait_ge(e_f, 1)
            act.activation(CA[:, 0, 0:T], CA[:, 1, 0:T], ACT.Abs).then_inc(e_a, 1)
            act.wait_ge(e_a, 1)
            act.activation(CA[:, 0, 0:T], CA[:, 0, 0:T], ACT.Exp, scale=-1.0).then_inc(e_a, 1)
            act.wait_ge(e_a, 2)
            act.activation(CA[:, 0, 0:T], CA[:, 0, 0:T], ACT.Ln, bias=ONES[0:8, 0:1]).then_inc(e_a, 1)
            for u in range(U_EVEN, U_EVEN + 8):
                hi_half(u + 2, u % 2, 0)
                hi_half(u + 2, u % 2, 1)
                if u < U_EVEN + 4:
                    for c in range(2):
                        n = 2 * (u - U_EVEN) + c
                        act.wait_ge(e_q, n + 1)
                        act.activation(SQT[:, n, :], QK[:, n, :], ACT.Square).then_inc(e_sq, 1)
            act.wait_ge(e_cr, 32)
            for n in range(8):
                act.wait_ge(s_hn, n + 1)
                act.activation(TF[:, n % 2, :], PS_[:, 6 + n % 2, :], ACT.Ln, bias=sc_(S_EPS), scale=1.0 / DH
                               ).then_inc(e_ln, 1)
                act.wait_ge(e_ln, n + 1)
                act.activation(SQT[:, n, :], TF[:, n % 2, :], ACT.Exp, scale=-0.5).then_inc(e_r, 1)
            with act.Fori(0, HEADS // 2) as pair:
                for h in range(2):
                    act.wait_ge(e_cr, 32)
                    act.wait_ge(a_qk, pair * 4 + (2 * h + 2))
                    act.activation(QS[64:65, h:h + 1, :], CR[64:65, ds(pair * 2 + h, 1), :], ACT.Copy).then_inc(a_row, 1)
                    act.activation(KS[96:97, h:h + 1, :], CR[96:97, ds(pair * 2 + h, 1), :], ACT.Copy).then_inc(a_row, 1)
                for s in range(9):
                    if s < 8:
                        n = (s % 4 + 1) * P
                        act.wait_ge(a_neg, pair * 8 + (s + 1))
                        if s >= 2:
                            act.wait_ge(a_t, pair * 8 + (s - 1))
                        act.activation(PR[:, s % 2, 0:n], PS_[:, 6 + s % 2, 0:n], ACT.Exp, bias=sc_(S_NM + s),
                                       accum_out=sc_(S_RS + s)).then_inc(a_e, 1)
                    if s >= 1:
                        n = ((s - 1) % 4 + 1) * P
                        act.wait_ge(a_t, pair * 8 + s)
                        if s >= 2:
                            act.wait_ge(a_o, pair * 8 + (s - 1))
                        act.activation(PT[:, 0:n], PS_[:, 4 + (s - 1) % 2, 0:n], ACT.Copy).then_inc(a_tc, 1)
            for c in range(4):
                act.wait_ge(a_ot, 16)
                act.activation(XH[:, c, :], PS_[:, c, :], ACT.Copy).then_inc(a_h, 1)
            for g in range(4):
                act.wait_ge(s_pm, g + 1)
                act.activation(XH[:, 4 + g, :], PS_[:, 4 + g, :], ACT.Copy, scale=col("pool_scale", g)).then_inc(e_ph, 1)
            for u in range(U_EOUT, U_EOUT + 4):
                hi_half(u + 2, u % 2, 0)
                hi_half(u + 2, u % 2, 1)
                for c in range(2):
                    n = 2 * (u - U_EOUT) + c
                    square(ST_F0, n, X[:, n, :])
            rms(ST_F0, 1.0 / D)

            def feed_forward(layer, next_stat):
                u = U_FFN[layer]
                t0 = 4 * 11 * layer
                for first, steps, kn in GROUPS:
                    with act.Fori(0, steps) as it:
                        for j, half in ((0, 0), (1, NG)):
                            hi_half(it * 2 + (u + 2 + j), j, 0)
                            for c in range(2):
                                z = it * 4 + (t0 + 4 * first + 2 * j + c + 1)
                                act.wait_ge(f_z, z)
                                if j == 1:
                                    act.wait_ge(f_s, it * 2 + (t0 // 2 + 2 * first + c + 1))
                                act.activation(TA[:, c, :], ZP[:, c, 2:T + 2], ACT.Identity,
                                               scale=col(f"fw{layer}2", it * 2 + (half + 2 * first + c)),
                                               bias=col(f"fb{layer}", it * 2 + (half + 2 * first + c))).then_inc(f_t, 1)
                            hi_half(it * 2 + (u + 2 + j), j, 1)
                            for c in range(2):
                                if j == 0:
                                    act.wait_ge(f_y, it * 8 + (2 * t0 + 8 * first + 3 + c))
                                    act.activation(TF[:, c, :], TA[:, c, :], ACT.Silu).then_inc(f_s, 1)
                                else:
                                    act.wait_ge(f_p, it * 2 + (t0 // 2 + 2 * first + c + 1))
                                    act.activation(HH[:, ds(it * 2 + c, 1), :], TF[:, c:c + 1, :], ACT.Copy).then_inc(f_h, 1)
                    u += 2 * steps
                    last = first + steps == 11
                    if not last:
                        with act.Fori(0, 2) as it:
                            for j in range(2):
                                hi_half(it * 2 + (u + 2 + j), j, 0)
                                hi_half(it * 2 + (u + 2 + j), j, 1)
                    else:
                        for v in range(u, u + 4):
                            if v + 2 < U_END:
                                hi_half(v + 2, v % 2, 0)
                                hi_half(v + 2, v % 2, 1)
                            if next_stat is not None:
                                for c in range(2):
                                    n = 2 * (v - u) + c
                                    square(next_stat, n, X[:, n, :])
                    u += 4

            split(3, "ffn_norm", 0)
            feed_forward(0, ST_X3)
            rms(ST_X3, 1.0 / D)
            split(4, "odd_norm", 0)
            with act.Fori(0, 4) as it:
                for j in range(2):
                    hi_half(it * 2 + (U_PW1 + 2 + j), j, 0)
                    hi_half(it * 2 + (U_PW1 + 2 + j), j, 1)
                    if j == 0:
                        for c in range(2):
                            act.wait_ge(g_c, it * 2 + (c + 1))
                            act.activation(TF[:, c, :], TA[:, c, :], ACT.Sigmoid).then_inc(g_s, 1)
            act.wait_ge(s_ss, ST_MEAN + 1)
            act.activation(R[:, :], PS_[:, ST_BANK, :], ACT.Copy, scale=1.0 / D).then_inc(n_m, 1)
            act.wait_ge(n_m, 1)
            act.activation(sc_(S_DUMP + 1), sc_(S_EPS), ACT.Copy).then_inc(s_ln, 1)
            act.activation(sc_(S_DUMP + 2), sc_(S_EPS), ACT.Copy).then_inc(s_r, 1)
            for c in range(DC):
                square(ST_VAR, c, CV[:, c, :])
            rms(ST_VAR, 1.0 / D)
            for c in range(DC):
                act.wait_ge(n_t, c + 1)
                act.activation(TF[:, c % 2, :], TA[:, c % 2, :], ACT.Silu, scale=col("ln_g", c), bias=col("ln_b", c)
                               ).then_inc(n_a, 1)
                act.wait_ge(n_a, c + 1)
                act.activation(XH[:, c, :], TF[:, c % 2, :], ACT.Copy).then_inc(n_h, 1)
            for u in range(U_PW2, U_PW2 + 4):
                hi_half(u + 2, u % 2, 0)
                hi_half(u + 2, u % 2, 1)
                for c in range(2):
                    n = 2 * (u - U_PW2) + c
                    square(ST_F1, n, X[:, n, :])
            rms(ST_F1, 1.0 / D)
            split(5, "ffn_norm", 8)
            feed_forward(1, None)
            for b in range(TB):
                act.wait_ge(s_yt, 2 * b + 2)
                act.activation(XROW[:, b, T:D], PS_[:, (2 * b + 1) % 4, :], ACT.Copy).then_inc(s_yc[1], 1)

        @block.vector
        def _(dve):
            tt, stt = dve.tensor_tensor, dve.scalar_tensor_tensor

            def lo_half(u, j, half, kn=8):
                dve.wait_ge(s_hi, u * 2 + (half + 1))
                a, b = (0, 4) if half == 0 else (4, kn)
                tt(WL[:, j, a:b, :], RAW[:, j, a:b, :], WH[:, j, a:b, :].bitcast(F32), ALU.subtract).then_inc(s_lo, 1)

            def clear_sum(stat):
                dve.memset(SQ[:, :], 0.0).then_inc(s_sqa, 1)

            def add_square(stat, m):
                dve.wait_ge(s_sqr, 8 * squares(stat) + m + 1)
                dve.wait_ge(s_sqa, 9 * stat + 1 + m)
                tt(SQ[:, :], SQ[:, :], TF[:, m % 2, :], ALU.add).then_inc(s_sqa, 1)

            def banks(j, c):
                return PS_[:, 2 * j + c, :]

            def mod_unit(a):
                dve.wait_ge(s_ar[a % 2], 16 * (a // 2 + 1))
                dst = MACC[:, a * UW:a * UW + UW]
                for k in range(8):
                    w, s = ARAW[:, a % 2, k, :], sc_(S_CS + k)
                    if k == 0:
                        dve.tensor_scalar(dst, w, s, None, ALU.mult).then_inc(s_as, 1)
                        continue
                    dve.wait_ge(s_as, 7 * a + k)
                    stt(dst, w, s, dst, ALU.mult, ALU.add).then_inc(s_as if k < 7 else s_ad, 1)

            def split(m, gs=None, gain=None, k=0):
                dve.wait_ge(s_r, (ST_X0, ST_X1, ST_X2, ST_F0, ST_X3, ST_F1)[m] + 1)

                def scaled(c):
                    tt(TA[:, c % 2, :], X[:, c, :], R[:, :], ALU.mult).then_inc(sp_t, 1)

                scaled(0)
                scaled(1)
                for c in range(DC):
                    dve.wait_ge(sp_h, 8 * m + c + 1)
                    if gain is None:
                        tt(XL[:, c, :], TF[:, c % 2, :], XH[:, c, :].bitcast(F32), ALU.subtract).then_inc(s_x, 1)
                    else:
                        stt(XL[:, c, :], TA[:, c % 2, :], col(gain, k + c), XH[:, c, :].bitcast(F32), ALU.mult,
                            ALU.subtract).then_inc(s_x, 1)
                    if c + 2 < DC:
                        if gain is not None:
                            dve.wait_ge(s_x, (0, 8, 16, 32, 40, 56)[m] + c + 1)
                        scaled(c + 2)

            def post_norm(stat, nth, gate):
                dve.wait_ge(s_r, stat + 1)
                clear_sum(stat + 1)
                for c in range(DC):
                    tt(TA[:, c % 2, :], Y[:, c, :], R[:, :], ALU.mult).then_inc(s_pn, 1)
                    dve.wait_ge(s_pn, 8 * nth + c + 1)
                    stt(X[:, c, :], TA[:, c % 2, :], sc_(gate + c), X[:, c, :], ALU.mult, ALU.add).then_inc(s_xu, 1)
                    if c >= 1:
                        add_square(stat + 1, c - 1)
                add_square(stat + 1, DC - 1)

            def residual_window(u, j, n, stat=None, dst=X, first=False, prep=True):
                dve.wait_ge(s_mm, u + 1)
                for c in range(2):
                    d = dst[:, ds(n + c, 1), :] if not isinstance(n, int) else dst[:, n + c:n + c + 1, :]
                    src = PS_[:, 2 * j + c:2 * j + c + 1, :]
                    ins = dve.tensor_copy(d, src) if first else tt(d, src, d, ALU.add)
                    if stat is not None:
                        ins.then_inc(s_xu, 1)
                    elif c == 1:
                        ins.then_inc(s_ev, 1)
                if stat is not None:
                    dve.wait_ge(s_xu, 8 * squares(stat) + n + 2)
                    dve.tensor_copy(sc_(S_DUMP), sc_(S_EPS)).then_inc(s_ev, 1)
                if prep:
                    lo_half(u + 2, j, 0)
                    lo_half(u + 2, j, 1)
                if stat is not None:
                    add_square(stat, n)
                    add_square(stat, n + 1)

            for t in range(VT):
                n = TILE_ROWS[t]
                dve.wait_ge(s_vt, t + 1)
                dve.tensor_copy(VCOL[:, TILE_COL[t]:TILE_COL[t] + n], PS_[:, 6 + t % 2, 0:n]).then_inc(s_ve, 1)
                if t == 0:
                    dve.wait_ge(s_const, 7)
                    clear_sum(ST_X0)
                    dve.wait_ge(s_cs, 1)
                    mod_unit(0)
                    mod_unit(1)
                    for c in range(DC):
                        dve.wait_ge(s_xt, c + 1)
                        dve.tensor_copy(X[:, c, :], PS_[:, c % 4, :]).then_inc(s_xe, 1)
                        dve.wait_ge(s_xe, c + 1)
                        dve.tensor_copy(sc_(S_DUMP), sc_(S_EPS)).then_inc(s_xu, 1)
                        if c >= 1:
                            add_square(ST_X0, c - 1)
                    add_square(ST_X0, DC - 1)
            for a in range(2, 8):
                mod_unit(a)
            for u in range(2):
                lo_half(u, u, 0)
                lo_half(u, u, 1)
            dve.wait_ge(s_ac, 1)
            tt(sc_(S_MOD, 16), PS_[:, COL_BANK, 0:16], col("ada_b", 0, 16), ALU.add).then_inc(s_sm, 1)
            dve.wait_ge(s_sm, 1)
            dve.wait_ge(s_ve, VT)
            stt(sc_(S_GS0, 8), sc_(S_MOD + 8, 8), 1.0, col("gains", 0, 8), ALU.add, ALU.mult).then_inc(s_sm, 1)
            dve.tensor_scalar(sc_(S_Q8), col("q_g"), DH ** -0.5, None, ALU.mult).then_inc(s_sm, 1)
            split(0)

            for u in range(12):
                step, j = u // 3, u % 2
                dve.wait_ge(s_mm, u + 1)
                if u % 3 == 0:
                    dve.tensor_copy(TF[:, 0, :], banks(j, 0))
                    dve.tensor_copy(TF[:, 1, :], banks(j, 1)).then_inc(s_ev, 1)
                elif u % 3 == 1:
                    dve.wait_ge(s_ev, u)
                    for c in range(2):
                        tt(ZP[:, c, 1:T + 1], banks(j, c), TF[:, c, :], ALU.mult).then_inc(c_z, 1)
                    dve.wait_ge(c_z, 2 * step + 2)
                    dve.tensor_copy(sc_(S_DUMP), sc_(S_EPS)).then_inc(s_ev, 1)
                    for tap, off in ((0, 0), (2, 2)):
                        for c in range(2):
                            n = 2 * step + c
                            if tap == 0:
                                dve.wait_ge(c_t, n + 1)
                            else:
                                dve.wait_ge(c_y, 4 * step + c + 1)
                            stt(TA[:, c, :], ZP[:, c, off:off + T], col("sc_conv", 8 * tap + n), TA[:, c, :],
                                ALU.mult, ALU.add).then_inc(c_y, 1)
                else:
                    for c in range(2):
                        dve.wait_ge(c_y, 4 * step + 3 + c)
                        tt(TA[:, c, :], banks(j, c), TA[:, c, :], ALU.mult).then_inc(c_g, 1)
                    dve.wait_ge(c_g, 2 * step + 2)
                    dve.tensor_copy(sc_(S_DUMP), sc_(S_EPS)).then_inc(s_ev, 1)
                lo_half(u + 2, j, 0)
                lo_half(u + 2, j, 1)
                if u % 3 == 2:
                    for c in range(2):
                        n = 2 * step + c
                        dve.wait_ge(c_h, n + 1)
                        tt(HL[:, n, :], TA[:, c, :], HH[:, n, :].bitcast(F32), ALU.subtract).then_inc(s_h, 1)
                mod_unit(8 + u)
            clear_sum(ST_Y0)
            for u in range(12, 16):
                residual_window(u, u % 2, 2 * (u - 12), ST_Y0, Y, first=True)
                mod_unit(8 + u)
            dve.wait_ge(s_ac, 2)
            tt(sc_(S_MOD + 16, 32), PS_[:, COL_BANK, 16:48], col("ada_b", 16, 32), ALU.add).then_inc(s_sm, 1)
            dve.wait_ge(s_sm, 4)
            tt(sc_(S_MG0, 8), sc_(S_MOD + 16, 8), col("gains", 8, 8), ALU.mult).then_inc(s_sm, 1)
            stt(sc_(S_GS1, 8), sc_(S_MOD + 32, 8), 1.0, col("gains", 16, 8), ALU.add, ALU.mult).then_inc(s_sm, 1)
            tt(sc_(S_MG1, 8), sc_(S_MOD + 40, 8), col("gains", 24, 8), ALU.mult).then_inc(s_sm, 1)
            dve.wait_ge(s_sm, 7)
            post_norm(ST_Y0, 0, S_MG0)
            dve.memset(Y[:, :, :], 0.0).then_inc(s_zero, 1)
            split(1)

            for g in range(4):
                with dve.Fori(0, 2) as it:
                    for j in range(2):
                        u = it * 2 + (U_MLP + 8 * g + j)
                        dve.wait_ge(s_mm, u + 1)
                        for c in range(2):
                            dve.tensor_scalar(TA[:, c, :], banks(j, c), 0.0, None, ALU.max).then_inc(m_r, 1)
                        dve.wait_ge(m_r, it * 4 + (8 * g + 2 * j + 2))
                        dve.tensor_copy(sc_(S_DUMP), sc_(S_EPS)).then_inc(s_ev, 1)
                        lo_half(u + 2, j, 0)
                        lo_half(u + 2, j, 1)
                        for c in range(2):
                            n = it * 4 + (2 * j + c)
                            dve.wait_ge(m_h, it * 4 + (8 * g + 2 * j + c + 1))
                            tt(HL[:, ds(n, 1), :], TF[:, c:c + 1, :], HH[:, ds(n, 1), :].bitcast(F32), ALU.subtract
                               ).then_inc(s_h, 1)
                if g < 3:
                    with dve.Fori(0, 2) as it:
                        for j in range(2):
                            residual_window(it * 2 + (U_MLP + 8 * g + 4 + j), j, it * 4 + 2 * j, None, Y)
            clear_sum(ST_Y1)
            for u in range(U_MLP + 28, U_MLP + 32):
                residual_window(u, u % 2, 2 * (u - U_MLP - 28), ST_Y1, Y)
            post_norm(ST_Y1, 1, S_MG1)
            dve.wait_ge(s_fh, 1)
            tt(FL[:, :, :], FRAW[:, :, :], FH[:, :, :].bitcast(F32), ALU.subtract).then_inc(s_fl, 1)
            split(2, gain="even_norm")

            dve.wait_ge(s_vin2, 16)
            dve.wait_ge(s_f, 1)
            dve.tensor_scalar(CA[:, 1, 0:T], PS_[0:8, COL_BANK, :], small[0:8, S_BF:S_BF + 1], None, ALU.add
                              ).then_inc(e_f, 1)
            dve.wait_ge(e_a, 3)
            stt(TF[0:8, 1, :], CA[:, 1, 0:T], 0.0, CA[:, 0, 0:T], ALU.min, ALU.subtract).then_inc(e_c, 1)
            dve.wait_ge(e_c, 1)
            dve.memset(CA[:, :, 0:256], 0.0)
            dve.tensor_copy(CA[:, 0, 256:256 + T], TF[0:8, 1, :]).then_inc(e_c, 1)
            for n in range(9):
                dve.wait_ge(e_c, n + 2)
                a, b = n % 2, (n + 1) % 2
                tt(CA[:, b, 256:256 + T], CA[:, a, 256:256 + T], CA[:, a, 256 - 2 ** n:256 + T - 2 ** n], ALU.add
                   ).then_inc(e_c, 1)
            dve.wait_ge(e_c, 11)
            dve.tensor_scalar(CA[:, 0, 256:256 + T], CA[:, 1, 256:256 + T], -1.0, None, ALU.mult).then_inc(e_c, 1)
            for u in range(U_EVEN, U_EVEN + 8):
                j, k = u % 2, u - U_EVEN
                dve.wait_ge(s_mm, u + 1)
                if k < 4:
                    for c in range(2):
                        dve.tensor_copy(QK[:, 2 * k + c, :], banks(j, c)).then_inc(e_q, 1)
                    dve.wait_ge(e_q, 2 * k + 2)
                    dve.tensor_copy(sc_(S_DUMP), sc_(S_EPS)).then_inc(s_ev, 1)
                elif k < 6:
                    for c in range(2):
                        ins = dve.tensor_copy(V[:, 2 * c:2 * c + 2, (k - 4) * UW:(k - 3) * UW],
                                              PS_[:, 2 * j + c, :].rearrange("p (b n) -> p b n", b=2))
                    ins.then_inc(s_ev, 1)
                else:
                    dve.wait_ge(s_zero, 2)
                    for c in range(2):
                        dve.tensor_copy(UP[:, 2 * (k - 6) + c, 16:], banks(j, c)).then_inc(e_u, 1)
                    dve.wait_ge(e_u, 2 * (k - 6) + 2)
                    dve.tensor_copy(sc_(S_DUMP), sc_(S_EPS)).then_inc(s_ev, 1)
                lo_half(u + 2, j, 0)
                lo_half(u + 2, j, 1)
            dve.wait_ge(e_r, 8)
            dve.wait_ge(s_f, 1)
            dve.memset(QS[64:97, :, :], 0.0).then_inc(s_zero, 1)
            dve.memset(KS[64:97, :, :], 0.0).then_inc(s_zero, 1)
            dve.wait_ge(s_zero, 4)
            dve.memset(QS[96:97, :, :], 1.0)
            dve.memset(KS[64:65, :, :], 1.0).then_inc(s_zero, 1)
            with dve.Fori(0, HEADS // 2) as pair:
                for h in range(2):
                    lo, hi = h * DH, h * DH + DH
                    stt(QS[0:DH, h:h + 1, :], QK[lo:hi, ds(pair, 1), :], small[lo:hi, S_Q8:S_Q8 + 1],
                        SQT[lo:hi, ds(pair, 1), :], ALU.mult, ALU.mult).then_inc(a_qk, 1)
                    stt(KS[0:DH, h:h + 1, :], QK[lo:hi, ds(pair + 4, 1), :], col("k_g")[lo:hi, :],
                        SQT[lo:hi, ds(pair + 4, 1), :], ALU.mult, ALU.mult).then_inc(a_qk, 1)
                for s in range(10):
                    if s < 8:
                        qb, n = s % 4, (s % 4 + 1) * P
                        S = PS_[:, 6 + s % 2, :]
                        dve.wait_ge(a_s, pair * 8 + (s + 1))
                        tt(S[:, n - P:n], S[:, n - P:n], MASK[:, :], ALU.add).then_inc(a_mask, 1)
                        dve.wait_ge(a_mask, pair * 8 + (s + 1))
                        dve.tensor_reduce(sc_(S_MX + s), S[:, 0:n], AX.X, ALU.max).then_inc(a_max, 1)
                        dve.wait_ge(a_max, pair * 8 + (s + 1))
                        dve.tensor_scalar(sc_(S_NM + s), sc_(S_MX + s), -1.0, None, ALU.mult).then_inc(a_neg, 1)
                    if 1 <= s < 9:
                        dve.wait_ge(a_e, pair * 8 + s)
                        dve.reciprocal(sc_(S_RR + s - 1), sc_(S_RS + s - 1)).then_inc(a_rr, 1)
                    if s >= 2:
                        k = s - 2
                        dve.wait_ge(a_o, pair * 8 + (k + 1))
                        dve.wait_ge(a_rr, pair * 8 + (k + 1))
                        dve.tensor_scalar(OT[:, k % 4, ds(pair * P + k // 4 * DH, DH)], PS_[:, k % 2, 0:DH],
                                          sc_(S_RR + k), None, ALU.mult).then_inc(a_oe, 1)
            for c in range(4):
                dve.wait_ge(a_h, c + 1)
                tt(XL[:, c, :], PS_[:, c, :], XH[:, c, :].bitcast(F32), ALU.subtract).then_inc(s_x, 1)
            dve.wait_ge(e_w, WINDOW_STEPS)
            for g, w in enumerate(WINDOWS):
                stt(UP[:, g, 16:], PS[:, g, :], 1.0 / w, UP[:, g, 16:], ALU.mult, ALU.subtract).then_inc(e_mx, 1)
            for g in range(4):
                dve.wait_ge(e_ph, g + 1)
                stt(XL[:, 4 + g, :], PS_[:, 4 + g, :], col("pool_scale", g), XH[:, 4 + g, :].bitcast(F32),
                    ALU.mult, ALU.subtract).then_inc(s_x, 1)
            clear_sum(ST_F0)
            for u in range(U_EOUT, U_EOUT + 4):
                residual_window(u, u % 2, 2 * (u - U_EOUT), ST_F0)

            def feed_forward(layer, next_stat):
                u = U_FFN[layer]
                t0 = 4 * 11 * layer
                dve.memset(ZP[:, :, 0:2], 0.0)
                for first, steps, kn in GROUPS:
                    with dve.Fori(0, steps) as it:
                        for j, half in ((0, 0), (1, NG)):
                            dve.wait_ge(s_mm, it * 2 + (u + 1 + j))
                            z = it * 4 + (t0 + 4 * first + 2 * j)
                            if j == 1:
                                dve.wait_ge(f_y, it * 8 + (2 * t0 + 8 * first + 4))
                            for c in range(2):
                                dve.tensor_copy(ZP[:, c, 2:T + 2], banks(j, c)).then_inc(f_z, 1)
                            lo_half(it * 2 + (u + 2 + j), j, 0)
                            dve.wait_ge(f_z, z + 2)
                            dve.tensor_copy(sc_(S_DUMP), sc_(S_EPS)).then_inc(s_ev, 1)
                            for tap in (1, 0):
                                for c in range(2):
                                    y = it * 8 + (2 * t0 + 8 * first + 4 * j)
                                    if tap == 1:
                                        dve.wait_ge(f_t, z + c + 1)
                                    else:
                                        dve.wait_ge(f_y, y + c + 1)
                                    stt(TA[:, c, :], ZP[:, c, tap:tap + T],
                                        col(f"fw{layer}{tap}", it * 2 + (half + 2 * first + c)), TA[:, c, :],
                                        ALU.mult, ALU.add).then_inc(f_y, 1)
                            if j == 1:
                                for c in range(2):
                                    dve.wait_ge(f_y, y + 3 + c)
                                    dve.wait_ge(f_s, it * 2 + (t0 // 2 + 2 * first + c + 1))
                                    tt(TF[:, c, :], TF[:, c, :], TA[:, c, :], ALU.mult).then_inc(f_p, 1)
                            lo_half(it * 2 + (u + 2 + j), j, 1)
                            if j == 1:
                                for c in range(2):
                                    n = it * 2 + c
                                    dve.wait_ge(f_h, it * 2 + (t0 // 2 + 2 * first + c + 1))
                                    tt(HL[:, ds(n, 1), :], TF[:, c:c + 1, :], HH[:, ds(n, 1), :].bitcast(F32),
                                       ALU.subtract).then_inc(s_h, 1)
                    u += 2 * steps
                    if first + steps < 11:
                        with dve.Fori(0, 2) as it:
                            for j in range(2):
                                residual_window(it * 2 + (u + j), j, it * 4 + 2 * j)
                    else:
                        if next_stat is not None:
                            clear_sum(next_stat)
                        for v in range(u, u + 4):
                            residual_window(v, v % 2, 2 * (v - u), next_stat, prep=v + 2 < U_END)
                    u += 4

            split(3, gain="ffn_norm")
            feed_forward(0, ST_X3)
            split(4, gain="odd_norm")

            dve.memset(UPAD[:, :, 0:PADU], 0.0).then_inc(s_zero, 1)
            with dve.Fori(0, 4) as it:
                for j in range(2):
                    u = it * 2 + (U_PW1 + j)
                    dve.wait_ge(s_mm, u + 1)
                    for c in range(2):
                        if j == 0:
                            dve.tensor_copy(TA[:, c, :], banks(j, c)).then_inc(g_c, 1)
                        else:
                            dve.wait_ge(g_s, it * 2 + (c + 1))
                            tt(UPAD[:, ds(it * 2 + c, 1), PADU:], PS_[:, 2 * j + c:2 * j + c + 1, :], TF[:, c:c + 1, :],
                               ALU.mult).then_inc(g_u, 1)
                    if j == 0:
                        dve.wait_ge(g_c, it * 2 + 2)
                    else:
                        dve.wait_ge(g_u, it * 2 + 2)
                    dve.tensor_copy(sc_(S_DUMP), sc_(S_EPS)).then_inc(s_ev, 1)
                    lo_half(u + 2, j, 0)
                    lo_half(u + 2, j, 1)
            dve.wait_ge(s_zero, 6)
            clear_sum(ST_MEAN)
            with dve.Fori(0, 4) as it:
                for tap in range(TAPS):
                    for c in range(2):
                        src = UPAD[:, ds(it * 2 + c, 1), tap:tap + T]
                        dst = CV[:, ds(it * 2 + c, 1), :]
                        if tap == 0:
                            dve.tensor_scalar(dst, src, col("dw_w0", it * 2 + c), col("dw_b", it * 2 + c), ALU.mult,
                                              ALU.add).then_inc(g_v, 1)
                        else:
                            dve.wait_ge(g_v, it * (2 * TAPS) + (2 * (tap - 1) + c + 1))
                            stt(dst, src, col("dw_w0", it * 2 + (8 * tap + c)), dst, ALU.mult, ALU.add).then_inc(g_v, 1)
                for c in range(2):
                    dve.wait_ge(g_v, it * (2 * TAPS) + (2 * (TAPS - 1) + c + 1))
                    dve.wait_ge(s_sqa, it * 2 + (9 * ST_MEAN + 1 + c))
                    tt(SQ[:, :].rearrange("p (a t) -> p a t", a=1), SQ[:, :].rearrange("p (a t) -> p a t", a=1),
                       CV[:, ds(it * 2 + c, 1), :], ALU.add).then_inc(s_sqa, 1)
            dve.wait_ge(n_m, 1)
            clear_sum(ST_VAR)
            for c in range(DC):
                tt(CV[:, c, :], CV[:, c, :], R[:, :], ALU.subtract).then_inc(s_xu, 1)
                if c >= 1:
                    add_square(ST_VAR, c - 1)
            add_square(ST_VAR, DC - 1)
            dve.wait_ge(s_r, ST_VAR + 1)

            def normed(c):
                tt(TA[:, c % 2, :], CV[:, c, :], R[:, :], ALU.mult).then_inc(n_t, 1)

            normed(0)
            normed(1)
            for c in range(DC):
                dve.wait_ge(n_h, c + 1)
                tt(XL[:, c, :], TF[:, c % 2, :], XH[:, c, :].bitcast(F32), ALU.subtract).then_inc(s_x, 1)
                if c + 2 < DC:
                    normed(c + 2)
            clear_sum(ST_F1)
            for u in range(U_PW2, U_PW2 + 4):
                residual_window(u, u % 2, 2 * (u - U_PW2), ST_F1)
            split(5, gain="ffn_norm", k=8)
            feed_forward(1, None)
            for b in range(TB):
                dve.wait_ge(s_yt, 2 * b + 1)
                dve.tensor_copy(XROW[:, b, 0:T], PS_[:, (2 * b) % 4, :]).then_inc(s_yc[0], 1)

        @block.tensor
        def _(pe):
            def product(u, j, mh, ml, kn=8, ready=None, base_=0):
                if not (isinstance(u, int) and u < 2):
                    pe.wait_ge(s_ev, u - 1)
                for k in range(kn):
                    if k == 0 or k == 4:
                        pe.wait_ge(s_lo, u * 2 + (k // 4 + 1))
                    pe.wait_ge(ready, base_ + k + 1)
                    for c in range(2):
                        wh, wl = (w[:, j, k, c * P:c * P + P] for w in (WH, WL))
                        o = PS_[:, 2 * j + c, :]
                        pe.matmul(o, wh, mh[:, k, :], start=(k == 0), stop=False)
                        pe.matmul(o, wh, ml[:, k, :], start=False, stop=False)
                        mm = pe.matmul(o, wl, mh[:, k, :], start=False, stop=(k == kn - 1))
                mm.then_inc(s_mm, 1)

            def x_units(u0, n, base_):
                with pe.Fori(0, n // 2) as it:
                    for j in range(2):
                        product(it * 2 + (u0 + j), j, XH, XL, 8, s_x, base_)

            def h_units(u0, n, base_, kn=8):
                with pe.Fori(0, n // 2) as it:
                    for j in range(2):
                        product(it * 2 + (u0 + j), j, HH, HL, kn, s_h, base_)

            def channel_sum(stat):
                pe.wait_ge(s_sqa, 9 * stat + 9)
                if stat:
                    pe.wait_ge(s_r, stat)
                pe.matmul(PS_[:, ST_BANK, :], ONES[:, :], SQ[:, :], start=True, stop=True).then_inc(s_ss, 1)

            pe.wait_ge(s_const, 7)
            pe.wait_ge(s_vin, 16 * (4 + 7 + 4 + 2 + 8))
            for t in range(VT):
                n = TILE_ROWS[t]
                if t >= 2:
                    pe.wait_ge(s_ve, t - 1)
                pe.transpose(PS_[:, 6 + t % 2, 0:n], VROW[0:n, t, :], IDENT[0:n, 0:n]).then_inc(s_vt, 1)
                if t == 0:
                    pe.wait_ge(s_xin, 16)
                    for c in range(DC):
                        if c >= 4:
                            pe.wait_ge(s_xe, c - 3)
                        for b in range(TB):
                            tr = pe.transpose(PS_[:, c % 4, b * P:b * P + P], XROW[:, b, c * P:c * P + P], IDENT[:, :])
                        tr.then_inc(s_xt, 1)
                    channel_sum(ST_X0)
            pe.wait_ge(s_ad, 8)
            for n in range(16):
                mm = pe.matmul(PS_[:, COL_BANK, n:n + 1], MACC[:, n * P:n * P + P], ONES[:, 0:1], start=True, stop=True)
            mm.then_inc(s_ac, 1)
            pe.wait_ge(s_xe, 8)
            for u in range(12):
                product(u, u % 2, XH, XL, 8, s_x, 0)
            for u in range(12, 16):
                product(u, u % 2, HH, HL, 8, s_h, 0)
            channel_sum(ST_Y0)
            pe.wait_ge(s_ad, 24)
            pe.wait_ge(s_sm, 1)
            for n in range(16, 48):
                mm = pe.matmul(PS_[:, COL_BANK, n:n + 1], MACC[:, n * P:n * P + P], ONES[:, 0:1], start=True, stop=True)
            mm.then_inc(s_ac, 1)
            channel_sum(ST_X1)
            for g in range(4):
                x_units(U_MLP + 8 * g, 4, 8)
                h_units(U_MLP + 8 * g + 4, 4, 8 + 8 * g)
            channel_sum(ST_Y1)
            channel_sum(ST_X2)
            pe.wait_ge(s_fl, 1)
            pe.wait_ge(s_sm, 4)
            for k in range(8):
                pe.wait_ge(s_x, 16 + k + 1)
                o = PS_[:, COL_BANK, :]
                pe.matmul(o, FH[:, k, :], XH[:, k, :], start=(k == 0), stop=False)
                pe.matmul(o, FH[:, k, :], XL[:, k, :], start=False, stop=False)
                mm = pe.matmul(o, FL[:, k, :], XH[:, k, :], start=False, stop=(k == 7))
            mm.then_inc(s_f, 1)
            x_units(U_EVEN, 4, 16)
            for j in range(2):
                u = U_EVEN + 4 + j
                pe.wait_ge(s_ev, u - 1)
                pe.wait_ge(s_lo, 2 * u + 2)
                for b in range(TB):
                    o = PS_[:, 2 * j + b // 2, b % 2 * UW:b % 2 * UW + UW]
                    for k in range(8):
                        xh, xl = (x[:, k, b * P:b * P + P] for x in (XH, XL))
                        pe.matmul(o, xh, WH[:, j, k, :], start=(k == 0), stop=False)
                        pe.matmul(o, xl, WH[:, j, k, :], start=False, stop=False)
                        mm = pe.matmul(o, xh, WL[:, j, k, :], start=False, stop=(k == 7))
                mm.then_inc(s_mm, 1)
            for j in range(2):
                product(U_EVEN + 6 + j, j, XH, XL, 8, s_x, 16)
            for n in range(8):
                pe.wait_ge(e_sq, n + 1)
                if n >= 2:
                    pe.wait_ge(e_ln, n - 1)
                pe.matmul(PS_[:, 6 + n % 2, :], BD[:, :], SQT[:, n, :], start=True, stop=True).then_inc(s_hn, 1)
            pe.wait_ge(s_zero, 5)
            pe.wait_ge(e_r, 8)
            pe.wait_ge(s_ev, U_EVEN + 8)
            with pe.Fori(0, HEADS // 2) as pair:
                for s in range(10):
                    if s < 8:
                        h, qb, n = s // 4, s % 4, (s % 4 + 1) * P
                        pe.wait_ge(a_qk, pair * 4 + 4)
                        pe.wait_ge(a_row, pair * 4 + 4)
                        if s >= 2:
                            pe.wait_ge(a_e, pair * 8 + (s - 1))
                        pe.matmul(PS_[:, 6 + s % 2, 0:n], QS[:, h, qb * P:qb * P + P], KS[:, h, 0:n], start=True,
                                  stop=True).then_inc(a_s, 1)
                    if 1 <= s < 9:
                        k = s - 1
                        pe.wait_ge(a_e, pair * 8 + (k + 1))
                        if k >= 2:
                            pe.wait_ge(a_tc, pair * 8 + (k - 1))
                        for b in range(k % 4 + 1):
                            tr = pe.transpose(PS_[:, 4 + k % 2, b * P:b * P + P], PR[:, k % 2, b * P:b * P + P], IDENT[:, :])
                        tr.then_inc(a_t, 1)
                    if s >= 2:
                        k = s - 2
                        pe.wait_ge(a_tc, pair * 8 + (k + 1))
                        if k >= 2:
                            pe.wait_ge(a_oe, pair * 8 + (k - 1))
                        for b in range(k % 4 + 1):
                            mm = pe.matmul(PS_[:, k % 2, 0:DH], PT[:, b * P:b * P + P],
                                           V[:, b, ds(pair * P + k // 4 * DH, DH)], start=(b == 0), stop=(b == k % 4))
                        mm.then_inc(a_o, 1)
            pe.wait_ge(a_oe, 32)
            for c in range(4):
                for b in range(TB):
                    pe.transpose(PS_[:, c, b * P:b * P + P], OT[:, b, c * P:c * P + P], IDENT[:, :]).then_inc(a_ot, 1)
            pe.wait_ge(s_wp, 16)
            for g in range(4):
                pe.wait_ge(e_mx, g + 1)
                pe.matmul(PS_[:, 4 + g, :], WP[:, g, :], UP[:, g, 16:], start=True, stop=True).then_inc(s_pm, 1)
            pe.wait_ge(s_x, 28)
            x_units(U_EOUT, 4, 24)
            channel_sum(ST_F0)

            def feed_forward(layer):
                u, h = U_FFN[layer], 40 + 22 * layer
                for first, steps, kn in GROUPS:
                    x_units(u, 2 * steps, 32 if layer == 0 else 56)
                    h_units(u + 2 * steps, 4, h + 2 * first, kn)
                    u += 2 * steps + 4

            feed_forward(0)
            channel_sum(ST_X3)
            x_units(U_PW1, 8, 40)
            channel_sum(ST_MEAN)
            channel_sum(ST_VAR)
            x_units(U_PW2, 4, 48)
            channel_sum(ST_F1)
            feed_forward(1)
            pe.wait_ge(s_ev, U_END)
            for n in range(2 * TB):
                if n >= 4:
                    pe.wait_ge(s_yc[n % 2], n // 2 - 1)
                for c in range(4):
                    tr = pe.transpose(PS_[:, n % 4, c * P:c * P + P], X[:, n % 2 * 4 + c, n // 2 * P:n // 2 * P + P],
                                      IDENT[:, :])
                tr.then_inc(s_yt, 1)


_INS = ["x", "c", "ada_w", "ada_b", "norm_gains", "mlp_w_in", "mlp_w_out", "sc_w_in", "sc_conv", "sc_w_out",
        "even_norm_g_2", "even_w_in_2", "even_b_f_2", "even_q_norm_g_2", "even_k_norm_g_2", "even_w_pool_2",
        "even_pool_scale_2", "even_w_out_2", "odd_norm_g_2", "odd_w_pw1_2", "odd_dw_w_2", "odd_dw_b_2",
        "odd_ln_g_2", "odd_ln_b_2", "odd_w_pw2_2", "ffn_norm_g_2", "ffn_w_up_2", "ffn_conv_w_2",
        "ffn_conv_b_2", "ffn_w_down_2"]


def kernel(**inputs):
    import numpy as _np
    import concourse.bacc as _bacc
    from concourse.bass_utils import run_bass_kernel_spmd as _run

    nc = _bacc.Bacc("TRN2", target_bir_lowering=False, num_devices=1)
    arrays, args = {}, {}
    for name in _INS:
        a = _np.ascontiguousarray(inputs[name])
        arrays[f"in_{name}"] = a
        args[name] = nc.dram_tensor(f"in_{name}", a.shape, mybir.dt.from_np(a.dtype), kind="ExternalInput").ap()
    out = nc.dram_tensor("out", (1, T, D), F32, kind="ExternalOutput").ap()
    program(nc, args, out)
    r = _run(nc, [arrays], core_ids=[0])
    return r.results[0]["out"]
```

```python
from contextlib import ExitStack

import concourse.bass as bass
from concourse import mybir

F32 = mybir.dt.float32
F32R = mybir.dt.float32r
ALU = mybir.AluOpType
ACT = mybir.ActivationFunctionType
AX = mybir.AxisListType
ds = bass.ds

P = 128
T = 512
TB = T // P
D = 1024
DC = D // P
F1 = 4 * D
F2 = 2816
NG = F2 // P
HEADS, DH = 8, 64
WINDOWS = (2, 4, 8, 16)
WINDOW_STEPS = sum(w.bit_length() - 1 + w - 1 for w in WINDOWS)
TAPS = 31
PADU = TAPS - 1
TAPS_PE = 10
TAPS_PE_LAST = 14
EPS = 1e-6
UW = 256
MASKED = 1e30

U_SCIN, U_SCOUT, U_MLP = 0, 12, 16
U_EVEN = U_MLP + 32
U_EOUT = U_EVEN + 8
U_PW1 = U_EOUT + 4 + 34
U_PW2 = U_PW1 + 8
U_FFN = (U_EOUT + 4, U_PW2 + 4)
U_END = U_FFN[1] + 34
GROUPS = ((0, 4, 8), (4, 4, 8), (8, 3, 6))

ROWS, TILE_ROWS = {}, []
for _names in ([("ada_b", 48), ("gains", 32), ("sc_conv", 24), ("c", 8)],
               [("even_norm", 8), ("odd_norm", 8), ("dw_b", 8), ("ln_g", 8), ("ln_b", 8),
                ("ffn_norm", 16), ("pool_scale", 4), ("q_g", 1), ("k_g", 1)],
               [("dw_w0", 124)], [("dw_w1", 124)],
               [("fw00", 44), ("fw01", 44)], [("fw02", 44), ("fb0", 44)],
               [("fw10", 44), ("fw11", 44)], [("fw12", 44), ("fb1", 44)]):
    _row = 0
    for _name, _n in _names:
        ROWS[_name] = (len(TILE_ROWS), _row)
        _row += _n
    TILE_ROWS.append(_row)
VT = len(TILE_ROWS)
TILE_COL = [sum(TILE_ROWS[:t]) for t in range(VT)]
S_EPS, S_BF, S_CS, S_MOD, S_DUMP = 0, 1, 2, 10, 58
S_MN, S_RS, S_RR = 112, 120, 128
S_GS0, S_MG0, S_GS1, S_MG1, S_Q8 = 66, 74, 82, 90, 98

ST_X0, ST_Y0, ST_X1, ST_Y1, ST_X2, ST_F0, ST_X3, ST_MEAN, ST_VAR, ST_F1 = range(10)


def summed(a):
    return (a // 2 + 1, (a + 1) // 2) if a < 8 else (a - 3, 4)


def window_mods(u):
    first = 8 + u + (u + 2) // 3
    return range(first, first + (2 if u % 3 == 0 else 1))


def squares(stat):
    return stat if stat <= ST_MEAN else stat - 1


def program(nc, i, out):
    ctx = ExitStack()
    with ctx:
        base = (nc.sbuf_base + 63) // 64 * 64

        def at(name, kib, shape, dt=F32):
            return nc.alloc_sbuf_tensor_at(name, shape, dt, offset=base + int(kib * 1024))

        def sem(name):
            return ctx.enter_context(nc.semaphore(name))

        X = at("X", 0, [P, DC, T])
        XH = at("XH", 16, [P, DC, T], F32R)
        XL = at("XL", 32, [P, DC, T], F32R)
        OT = at("OT", 16, [P, TB, T])
        PS = at("PS", 24, [P, 4, T])
        HH = at("HH", 48, [P, 8, T], F32R)
        HL = at("HL", 64, [P, 8, T], F32R)
        VROW = at("VROW", 48, [P, VT, P])
        CR = at("CR", 48, [97, HEADS, T])
        UP = at("UP", 64, [P, 4, 16 + T])
        PA = at("PA", 72.5, [P, 2, 16 + T])
        RAW = at("RAW", 80, [P, 2, 8, UW])
        WH = at("WH", 96, [P, 2, 8, UW], F32R)
        WL = at("WL", 112, [P, 2, 8, UW], F32R)
        Y = at("Y", 128, [P, DC, T])
        XROW = at("XROW", 128, [P, TB, D])
        QK = at("QK", 128, [P, 8, T])
        UPAD = at("UPAD", 128, [P, DC, PADU + T])
        VCOL = at("VCOL", 145, [P, sum(TILE_ROWS)])
        MACC = at("MACC", 148.5, [P, 6 * D])
        SQT = at("SQT", 148.5, [P, 8, T])
        V = at("V", 164.5, [P, TB, T])
        CV = at("CV", 148.5, [P, DC, T])
        ARAW = at("ARAW", 172.5, [P, 2, 8, UW])
        FRAW = at("FRAW", 172.5, [P, 8, P])
        FH = at("FH", 176.5, [P, 8, P], F32R)
        FL = at("FL", 180.5, [P, 8, P], F32R)
        DG = at("DG", 172.5, [P, 2, TAPS_PE_LAST, P])
        WP = at("WP", 184.5, [P, 4, P])
        QS = at("QS", 172.5, [97, 2, T])
        KS = at("KS", 176.5, [97, 2, T])
        PR = at("PR", 180.5, [P, 2, T])
        PT = at("PT", 188.5, [P, 2, T])
        TA = at("TA", 188.5, [P, 2, T])
        TF = at("TF", 192.5, [P, 2, T])
        CA = at("CA", 188.5, [8, 2, 256 + T])
        ZP = at("ZP", 196.5, [P, 2, 2 + T])
        R = at("R", 200.75, [P, T])
        SQ = at("SQ", 202.75, [P, T])
        IDENT = at("IDENT", 204.75, [P, P])
        ONES = at("ONES", 205.25, [P, P])
        BD = at("BD", 205.75, [P, P])
        MASK = at("MASK", 206.25, [P, P])
        small = at("small", 206.75, [P, 136])
        PS_ = ctx.enter_context(nc.psum_tensor("PSUM", [P, 8, T], F32))
        ST_BANK, COL_BANK = 4, 5
        S_BANKS = (2, 3, 6, 7)

        def col(name, k=0, n=1):
            t, r = ROWS[name]
            return VCOL[:, ds(k + (TILE_COL[t] + r), n)] if not isinstance(k, int) else \
                VCOL[:, TILE_COL[t] + r + k:TILE_COL[t] + r + k + n]

        def sc_(k, n=1):
            return small[:, k:k + n]

        s_raw = [sem("unit_loaded_even"), sem("unit_loaded_odd")]
        s_hi, s_lo = sem("half_unit_hi"), sem("half_unit_lo")
        s_mm, s_ev = sem("unit_multiplied"), sem("unit_banks_emptied")
        s_x, s_h = sem("input_chunk_ready"), sem("hidden_chunk_ready")
        s_xin = sem("x_rows_loaded")
        s_vin0, s_vin, s_vin2 = sem("first_vectors_loaded"), sem("vectors_loaded"), sem("bf_loaded")
        s_const, s_const0 = sem("constants_ready"), sem("constants_cleared")
        s_xt, s_xe, s_vt, s_ve = sem("x_turned"), sem("x_copied"), sem("vectors_turned"), sem("vectors_copied")
        s_cs, s_sm = sem("silu_c"), sem("small_vector_step")
        s_ar = [sem("mod_weights_even"), sem("mod_weights_odd")]
        s_ad, s_as, s_ap = sem("mod_unit_summed"), sem("mod_step"), sem("mod_unit_multiplied")
        s_ac = sem("mod_columns")
        s_xu, s_sqr, s_sqa = sem("chunk_to_square"), sem("chunk_squared"), sem("square_sum_step")
        s_ss, s_ln, s_r = sem("channel_sum"), sem("ln_of_sum"), sem("rms_ready")
        sp_t, sp_y, sp_h = sem("split_scaled"), sem("split_shifted"), sem("split_hi")
        s_pn = sem("postnorm_scaled")
        c_z, c_t, c_y, c_g, c_h = (sem("gconv_" + x) for x in ("cv", "centre", "taps", "gated", "hi"))
        m_r, m_f, m_h = (sem("mlp_" + x) for x in ("relu", "squared", "hi"))
        f_z, f_t, f_y, f_s, f_p, f_h = (sem("ffn_" + x) for x in ("z", "centre", "taps", "silu", "product", "hi"))
        s_fw, s_fh, s_fl, s_f = sem("forget_w"), sem("forget_w_hi"), sem("forget_w_lo"), sem("forget_logits")
        e_f, e_a, e_c, e_cr = sem("logit_biased"), sem("logit_act"), sem("cumsum_step"), sem("decay_rows")
        e_q, e_sq, s_hn, e_ln, e_r = (sem("qk_" + x) for x in ("chunk", "squared", "head_sum", "ln", "rms"))
        e_u, e_w = sem("pool_input"), sem("window_step")
        s_wp, e_mx, s_pm, e_ph = sem("pool_w"), sem("pool_mixed"), sem("pool_product"), sem("pool_hi")
        a_qk, a_row = sem("head_qk"), sem("head_decay_rows")
        a_s, a_min, a_e, a_rr = (sem("attn_" + x) for x in ("scores", "min", "exp", "recip"))
        a_t, a_tc, a_o, a_oe = (sem("attn_" + x) for x in ("turned", "copied", "out", "out_copied"))
        a_ot, a_h = sem("attn_out_turned"), sem("attn_out_hi")
        g_c, g_s, g_u, g_v, g_o, g_d, g_m, g_a = (sem("conf_" + x) for x in
                                             ("gate", "sigmoid", "input", "tap", "odd_taps_added", "diagonals",
                                              "taps_pe", "taps_added"))
        n_m, n_c, n_t, n_a, n_y, n_h = (sem("ln_" + x) for x in ("mean", "centred", "scaled", "silu", "y", "hi"))
        s_zero = sem("pads_cleared")
        s_yt, s_out = sem("out_turned"), sem("out_stored")
        s_yc = [sem("out_copied_left"), sem("out_copied_right")]

        block = ctx.enter_context(nc.Block())

        def wview(name, layer=0):
            return i[name][layer].rearrange("(k p) n -> p k n", p=P)

        @block.sync
        def _(sp):
            def load(u, j, w, c0, k0=0, kn=8):
                if not (isinstance(u, int) and u < 2):
                    sp.wait_ge(s_lo, u * 2 - 2)
                sp.dma_start(RAW[:, j, 0:kn, :], w[:, k0:k0 + kn, ds(c0, UW)]).then_inc(s_raw[j], 16)

            def load_mod(a):
                if a in (3, 5, 7, 9):
                    sp.wait_ge(s_ap, summed(a - 2)[1])
                elif a >= 2:
                    sp.wait_ge(s_ad, summed(a - 2)[0])
                sp.dma_start(ARAW[:, a % 2], ada[:, :, a * UW:a * UW + UW]).then_inc(s_ar[a % 2], 16)

            ada = wview("ada_w")
            x_rows = i["x"][0].rearrange("(b p) d -> p b d", p=P)
            def rows(name, ap, n):
                t, r = ROWS[name]
                sp.dma_start(VROW[r:r + n, t, :], ap).then_inc(s_vin if t else s_vin0, 16)

            def r128(ap):
                return ap.rearrange("(r p) -> r p", p=P)

            rows("c", r128(i["c"][0]), 8)
            rows("ada_b", r128(i["ada_b"][0]), 48)
            rows("gains", i["norm_gains"][0].rearrange("g (r p) -> (g r) p", p=P), 32)
            rows("sc_conv", i["sc_conv"][0].rearrange("g (r p) -> (g r) p", p=P), 24)
            load_mod(0)
            load_mod(1)
            sp.dma_start(XROW[:, :, :], x_rows).then_inc(s_xin, 16)
            rows("even_norm", r128(i["even_norm_g_2"][0]), 8)
            rows("odd_norm", r128(i["odd_norm_g_2"][0]), 8)
            rows("dw_b", r128(i["odd_dw_b_2"][0]), 8)
            rows("ln_g", r128(i["odd_ln_g_2"][0]), 8)
            rows("ln_b", r128(i["odd_ln_b_2"][0]), 8)
            rows("ffn_norm", i["ffn_norm_g_2"].rearrange("g (r p) -> (g r) p", p=P), 16)
            rows("pool_scale", r128(i["even_pool_scale_2"][0]), 4)
            for name in ("q", "k"):
                t, r = ROWS[name + "_g"]
                for half in range(2):
                    sp.dma_start(VROW[r:r + 1, t, half * DH:half * DH + DH], i[f"even_{name}_norm_g_2"]
                                 ).then_inc(s_vin, 16)
            dw = i["odd_dw_w_2"][0].rearrange("g (r p) -> (g r) p", p=P)
            rows("dw_w0", dw[0:124], 124)
            rows("dw_w1", dw[124:248], 124)
            for layer in range(2):
                for tap in range(3):
                    rows(f"fw{layer}{tap}", r128(i["ffn_conv_w_2"][layer, tap]), 2 * NG)
                rows(f"fb{layer}", r128(i["ffn_conv_b_2"][layer]), 2 * NG)
            sp.dma_start(small[0:8, S_BF:S_BF + 1], i["even_b_f_2"].rearrange("a h -> h a")).then_inc(s_vin2, 16)

            scin, scout = wview("sc_w_in"), wview("sc_w_out")
            order = (D, 2 * D, 0)
            load(0, 0, scin, order[0])
            load(1, 1, scin, order[1])
            for a in range(2, 8):
                load_mod(a)
            for u in range(2, 16):
                if u < 12:
                    load(u, u % 2, scin, order[u % 3] + u // 3 * UW)
                else:
                    load(u, u % 2, scout, (u - 12) * UW)
                if u < 4:
                    load_mod(6 + u)
                else:
                    for a in window_mods(u - 4):
                        if a + 2 < 24:
                            load_mod(a + 2)
            w_in, w_out = wview("mlp_w_in"), wview("mlp_w_out")
            for g in range(4):
                with sp.Fori(0, 2) as it:
                    for j in range(2):
                        load(it * 2 + (U_MLP + 8 * g + j), j, w_in, it * (2 * UW) + (g * D + j * UW))
                with sp.Fori(0, 2) as it:
                    for j in range(2):
                        load(it * 2 + (U_MLP + 8 * g + 4 + j), j, w_out, it * (2 * UW) + j * UW, 8 * g)
            ein = wview("even_w_in_2")
            sp.wait_ge(s_ad, 20)
            sp.dma_start(FRAW[:, :, :], ein[:, :, 1536:1536 + P]).then_inc(s_fw, 16)
            sp.dma_start(WP[:, :, :], i["even_w_pool_2"][0].rearrange("g c d -> c g d")).then_inc(s_wp, 16)
            with sp.Fori(0, 3) as it:
                for j in range(2):
                    load(it * 2 + (U_EVEN + j), j, ein, it * (2 * UW) + j * UW)
            for j in range(2):
                load(U_EVEN + 6 + j, j, ein, 1544 + j * UW)
            eout = wview("even_w_out_2")
            load(U_EOUT, 0, eout, 0)
            load(U_EOUT + 1, 1, eout, UW)
            sp.wait_ge(e_c, 11)
            sp.dma_start(CR[64:65, :, :], CA[:, 1, 256:256 + T]).then_inc(e_cr, 16)
            sp.dma_start(CR[96:97, :, :], CA[:, 1, 256:256 + T]).then_inc(e_cr, 16)
            load(U_EOUT + 2, 0, eout, 2 * UW)
            load(U_EOUT + 3, 1, eout, 3 * UW)

            def feed_forward(layer):
                up, down = wview("ffn_w_up_2", layer), wview("ffn_w_down_2", layer)
                u = U_FFN[layer]
                for first, steps, kn in GROUPS:
                    with sp.Fori(0, steps) as it:
                        load(it * 2 + u, 0, up, it * UW + first * UW)
                        load(it * 2 + (u + 1), 1, up, it * UW + (F2 + first * UW))
                    u += 2 * steps
                    with sp.Fori(0, 2) as it:
                        for j in range(2):
                            load(it * 2 + (u + j), j, down, it * (2 * UW) + j * UW, 2 * first, kn)
                    u += 4

            feed_forward(0)
            pw1, pw2 = wview("odd_w_pw1_2"), wview("odd_w_pw2_2")
            with sp.Fori(0, 4) as it:
                load(it * 2 + U_PW1, 0, pw1, it * UW + D)
                load(it * 2 + (U_PW1 + 1), 1, pw1, it * P + it * P)
            with sp.Fori(0, 2) as it:
                for j in range(2):
                    load(it * 2 + (U_PW2 + j), j, pw2, it * (2 * UW) + j * UW)
            feed_forward(1)
            for b in range(TB):
                sp.wait_ge(s_yc[0], b + 1)
                sp.wait_ge(s_yc[1], b + 1)
                sp.dma_start(out[0, b * P:b * P + P, :], XROW[:, b, :]).then_inc(s_out, 16)
            sp.wait_ge(s_out, 16 * TB)

        @block.gpsimd
        def _(pool):
            for m, v in ((IDENT, 0.0), (ONES, 1.0), (BD, 0.0), (MASK, 0.0)):
                pool.memset(m[:, :], v).then_inc(s_const0, 1)
            pool.memset(sc_(S_EPS), EPS).then_inc(s_const, 1)
            pool.wait_ge(s_const0, 4)
            pool.affine_select(out=IDENT[:, :], in_=IDENT[:, :], compare_op=ALU.not_equal, fill=1.0, base=0,
                               pattern=[[-1, P]], channel_multiplier=1).then_inc(s_const, 1)
            pool.affine_select(out=MASK[:, :], in_=MASK[:, :], compare_op=ALU.is_ge, fill=MASKED, base=0,
                               pattern=[[-1, P]], channel_multiplier=1).then_inc(s_const, 1)
            for h in range(2):
                pool.wait_ge(s_const, 3 + h)
                pool.memset(BD[h * DH:h * DH + DH, h * DH:h * DH + DH], 1.0).then_inc(s_const, 1)
            pool.wait_ge(s_const, 5)
            pool.memset(ZP[:, :, 0:1], 0.0).then_inc(s_const, 1)
            pool.wait_ge(s_const, 6)
            pool.memset(ZP[:, :, T + 1:T + 2], 0.0).then_inc(s_const, 1)

            pool.wait_ge(s_mm, U_MLP + 32)
            pool.memset(UP[:, :, 0:16], 0.0).then_inc(s_zero, 1)
            pool.wait_ge(e_u, 4)
            pool.wait_ge(s_mm, U_EVEN + 8)
            step = 0
            for g, w in enumerate(WINDOWS):
                src, have = UP[:, g, :], 1
                while have < w:
                    last = 2 * have == w
                    lo = 16 if last else 2 * have - 1
                    dst = PS[:, g, :] if last else PA[:, step % 2, lo:]
                    if step:
                        pool.wait_ge(e_w, step)
                    pool.tensor_tensor(dst, src[:, lo:], src[:, lo - have:16 + T - have], ALU.add).then_inc(e_w, 1)
                    src, have, step = PA[:, step % 2, :], 2 * have, step + 1
            for g, w in enumerate(WINDOWS):
                for t in range(w - 1):
                    pool.wait_ge(e_w, step)
                    pool.tensor_scalar(PS[:, g, t:t + 1], PS[:, g, t:t + 1], float(w) / (t + 1), 0.0,
                                       ALU.mult, ALU.add).then_inc(e_w, 1)
                    step += 1

        @block.scalar
        def _(act):
            def hi_half(u, j, half, kn=8):
                if half == 0:
                    if not (isinstance(u, int) and u < 2):
                        act.wait_ge(s_mm, u - 1)
                    act.wait_ge(s_raw[j], (u - j) * 8 + 16)
                a, b = (0, 4) if half == 0 else (4, kn)
                act.activation(WH[:, j, a:b, :], RAW[:, j, a:b, :], ACT.Copy).then_inc(s_hi, 1)

            def prep_late(u):
                hi_half(u, 1, 0)
                hi_half(u, 1, 1)

            def square(stat, m, src):
                q = 8 * squares(stat) + m
                act.wait_ge(s_xu, q + 1)
                if m_at_least(m, 2):
                    act.wait_ge(s_sqa, m + (9 * stat))
                act.activation(TF[:, m % 2 if isinstance(m, int) else 0, :], src, ACT.Square).then_inc(s_sqr, 1)

            def m_at_least(m, n):
                return not isinstance(m, int) or m >= n

            def rms(stat, scale):
                act.wait_ge(s_ss, stat + 1)
                act.activation(R[:, :], PS_[:, ST_BANK, :], ACT.Ln, bias=sc_(S_EPS), scale=scale).then_inc(s_ln, 1)
                act.wait_ge(s_ln, stat + 1)
                act.activation(R[:, :], R[:, :], ACT.Exp, scale=-0.5).then_inc(s_r, 1)

            def split_shift(m, gs, sh):
                for c in range(DC):
                    act.wait_ge(sp_t, 8 * m + c + 1)
                    act.activation(TF[:, c % 2, :], TA[:, c % 2, :], ACT.Identity, scale=sc_(gs + c),
                                   bias=sc_(sh + c)).then_inc(sp_y, 1)
                    act.wait_ge(sp_y, 8 * m + c + 1)
                    act.activation(XH[:, c, :], TF[:, c % 2, :], ACT.Copy).then_inc(sp_h, 1)

            def split(m, gain, k):
                for c in range(DC):
                    act.wait_ge(sp_t, 8 * m + c + 1)
                    act.activation(XH[:, c, :], TA[:, c % 2, :], ACT.Copy, scale=col(gain, k + c)).then_inc(sp_h, 1)

            act.wait_ge(s_ve, 1)
            act.activation(sc_(S_CS, 8), col("c", 0, 8), ACT.Silu).then_inc(s_cs, 1)
            for c in range(DC):
                square(ST_X0, c, X[:, c, :])
            act.wait_ge(s_const, 1)
            rms(ST_X0, 1.0 / D)
            for u in range(2):
                hi_half(u, u, 0)
                hi_half(u, u, 1)
            act.wait_ge(s_sm, 3)
            split_shift(0, S_GS0, S_MOD)

            for u in range(12):
                hi_half(u + 2, u % 2, 0)
                step = u // 3
                if u % 3 == 1:
                    for c in range(2):
                        n = 2 * step + c
                        act.wait_ge(c_z, n + 1)
                        act.activation(TA[:, c, :], ZP[:, c, 1:T + 1], ACT.Copy, scale=col("sc_conv", 8 + n)
                                       ).then_inc(c_t, 1)
                hi_half(u + 2, u % 2, 1)
                if u % 3 == 2:
                    for c in range(2):
                        n = 2 * step + c
                        act.wait_ge(c_g, n + 1)
                        act.activation(HH[:, n, :], TA[:, c, :], ACT.Copy).then_inc(c_h, 1)
            for u in range(12, 16):
                if u < 15:
                    hi_half(u + 2, u % 2, 0)
                    hi_half(u + 2, u % 2, 1)
                for c in range(2):
                    n = 2 * (u - 12) + c
                    square(ST_Y0, n, Y[:, n, :])
            rms(ST_Y0, 1.0 / D)
            for c in range(DC):
                square(ST_X1, c, X[:, c, :])
            rms(ST_X1, 1.0 / D)
            split_shift(1, S_GS1, S_MOD + 24)
            prep_late(U_MLP + 1)

            for g in range(4):
                with act.Fori(0, 2) as it:
                    for j in range(2):
                        u = it * 2 + (U_MLP + 8 * g + j)
                        hi_half(u + 2, j, 0)
                        for c in range(2):
                            act.wait_ge(m_r, it * 4 + (8 * g + 2 * j + c + 1))
                            act.activation(TF[:, c, :], TA[:, c, :], ACT.Square).then_inc(m_f, 1)
                        hi_half(u + 2, j, 1)
                        for c in range(2):
                            act.wait_ge(m_f, it * 4 + (8 * g + 2 * j + c + 1))
                            act.activation(HH[:, ds(it * 4 + (2 * j + c), 1), :], TF[:, c:c + 1, :], ACT.Copy
                                           ).then_inc(m_h, 1)
                if g < 3:
                    with act.Fori(0, 2) as it:
                        for j in range(2):
                            u = it * 2 + (U_MLP + 8 * g + 4 + j)
                            hi_half(u + 2, j, 0)
                            hi_half(u + 2, j, 1)
            for u in range(U_MLP + 28, U_MLP + 32):
                if u < U_MLP + 31:
                    hi_half(u + 2, u % 2, 0)
                    hi_half(u + 2, u % 2, 1)
                for c in range(2):
                    n = 2 * (u - U_MLP - 28) + c
                    square(ST_Y1, n, Y[:, n, :])
            rms(ST_Y1, 1.0 / D)
            for c in range(DC):
                square(ST_X2, c, X[:, c, :])
            rms(ST_X2, 1.0 / D)
            act.wait_ge(s_fw, 16)
            act.activation(FH[:, :, :], FRAW[:, :, :], ACT.Copy).then_inc(s_fh, 1)
            split(2, "even_norm", 0)
            prep_late(U_EVEN + 1)

            act.wait_ge(e_f, 1)
            act.activation(CA[:, 0, 0:T], CA[:, 1, 0:T], ACT.Abs).then_inc(e_a, 1)
            act.wait_ge(e_a, 1)
            act.activation(CA[:, 0, 0:T], CA[:, 0, 0:T], ACT.Exp, scale=-1.0).then_inc(e_a, 1)
            act.wait_ge(e_a, 2)
            act.activation(CA[:, 0, 0:T], CA[:, 0, 0:T], ACT.Ln, bias=ONES[0:8, 0:1]).then_inc(e_a, 1)
            for u in range(U_EVEN, U_EVEN + 8):
                hi_half(u + 2, u % 2, 0)
                hi_half(u + 2, u % 2, 1)
                if u < U_EVEN + 4:
                    for c in range(2):
                        n = 2 * (u - U_EVEN) + c
                        act.wait_ge(e_q, n + 1)
                        act.activation(SQT[:, n, :], QK[:, n, :], ACT.Square).then_inc(e_sq, 1)
                else:
                    n0 = 2 * (u - U_EVEN - 4)
                    if n0 == 6:
                        act.wait_ge(e_cr, 32)
                    for n in (n0, n0 + 1):
                        act.wait_ge(s_hn, n + 1)
                        act.activation(SQT[:, n, :], PS_[:, 6 + n % 2, :], ACT.Ln, bias=sc_(S_EPS), scale=1.0 / DH
                                       ).then_inc(e_ln, 1)
                    for n in (n0, n0 + 1):
                        act.wait_ge(e_ln, n + 1)
                        act.activation(SQT[:, n, :], SQT[:, n, :], ACT.Exp, scale=-0.5).then_inc(e_r, 1)
            with act.Fori(0, HEADS // 2) as pair:
                for h in range(2):
                    act.wait_ge(e_cr, 32)
                    act.wait_ge(a_qk, pair * 4 + (2 * h + 2))
                    act.activation(QS[64:65, h:h + 1, :], CR[64:65, ds(pair * 2 + h, 1), :], ACT.Copy).then_inc(a_row, 1)
                    act.activation(KS[96:97, h:h + 1, :], CR[96:97, ds(pair * 2 + h, 1), :], ACT.Copy).then_inc(a_row, 1)
                for s in range(10):
                    if s < 8:
                        n = (s % 4 + 1) * P
                        act.wait_ge(a_min, pair * 8 + (s + 1))
                        if s >= 2:
                            act.wait_ge(a_t, pair * 8 + (s - 1))
                        act.activation(PR[:, s % 2, 0:n], PS_[:, S_BANKS[s % 4], 0:n], ACT.Exp, scale=-1.0,
                                       bias=sc_(S_MN + s), accum_out=sc_(S_RS + s)).then_inc(a_e, 1)
                    if s >= 2:
                        k, n = s - 2, ((s - 2) % 4 + 1) * P
                        act.wait_ge(a_t, pair * 8 + (k + 1))
                        if k >= 2:
                            act.wait_ge(a_o, pair * 8 + (k - 1))
                        act.activation(PT[:, k % 2, 0:n], PS_[:, 4 + k % 2, 0:n], ACT.Copy).then_inc(a_tc, 1)
            for c in range(4):
                act.wait_ge(a_ot, 16)
                act.activation(XH[:, c, :], PS_[:, c, :], ACT.Copy).then_inc(a_h, 1)
            for g in range(4):
                act.wait_ge(s_pm, g + 1)
                act.activation(XH[:, 4 + g, :], PS_[:, 4 + g, :], ACT.Copy, scale=col("pool_scale", g)).then_inc(e_ph, 1)
            for u in range(U_EOUT, U_EOUT + 4):
                if u < U_EOUT + 3:
                    hi_half(u + 2, u % 2, 0)
                    hi_half(u + 2, u % 2, 1)
                for c in range(2):
                    n = 2 * (u - U_EOUT) + c
                    square(ST_F0, n, X[:, n, :])
            rms(ST_F0, 1.0 / D)

            def feed_forward(layer, next_stat):
                u = U_FFN[layer]
                t0 = 4 * 11 * layer
                for first, steps, kn in GROUPS:
                    with act.Fori(0, steps) as it:
                        for j, half in ((0, 0), (1, NG)):
                            hi_half(it * 2 + (u + 2 + j), j, 0)
                            for c in range(2):
                                z = it * 4 + (t0 + 4 * first + 2 * j + c + 1)
                                act.wait_ge(f_z, z)
                                if j == 1:
                                    act.wait_ge(f_s, it * 2 + (t0 // 2 + 2 * first + c + 1))
                                act.activation(TA[:, c, :], ZP[:, c, 2:T + 2], ACT.Identity,
                                               scale=col(f"fw{layer}2", it * 2 + (half + 2 * first + c)),
                                               bias=col(f"fb{layer}", it * 2 + (half + 2 * first + c))).then_inc(f_t, 1)
                            hi_half(it * 2 + (u + 2 + j), j, 1)
                            for c in range(2):
                                if j == 0:
                                    act.wait_ge(f_y, it * 8 + (2 * t0 + 8 * first + 3 + c))
                                    act.activation(TF[:, c, :], TA[:, c, :], ACT.Silu).then_inc(f_s, 1)
                                else:
                                    act.wait_ge(f_p, it * 2 + (t0 // 2 + 2 * first + c + 1))
                                    act.activation(HH[:, ds(it * 2 + c, 1), :], TF[:, c:c + 1, :], ACT.Copy).then_inc(f_h, 1)
                    u += 2 * steps
                    last = first + steps == 11
                    if not last:
                        with act.Fori(0, 2) as it:
                            for j in range(2):
                                hi_half(it * 2 + (u + 2 + j), j, 0)
                                hi_half(it * 2 + (u + 2 + j), j, 1)
                    else:
                        for v in range(u, u + 4):
                            if v + 2 < U_END and not (next_stat is not None and v == u + 3):
                                hi_half(v + 2, v % 2, 0)
                                hi_half(v + 2, v % 2, 1)
                            if next_stat is not None:
                                for c in range(2):
                                    n = 2 * (v - u) + c
                                    square(next_stat, n, X[:, n, :])
                    u += 4

            split(3, "ffn_norm", 0)
            prep_late(U_FFN[0] + 1)
            feed_forward(0, ST_X3)
            rms(ST_X3, 1.0 / D)
            split(4, "odd_norm", 0)
            prep_late(U_PW1 + 1)
            def gate_unit(it):
                u = it * 2 + U_PW1
                hi_half(u + 2, 0, 0)
                hi_half(u + 2, 0, 1)
                for c in range(2):
                    act.wait_ge(g_c, it * 2 + (c + 1))
                    act.activation(TF[:, c, :], TA[:, c, :], ACT.Sigmoid).then_inc(g_s, 1)

            def value_unit(it):
                hi_half(it * 2 + (U_PW1 + 3), 1, 0)
                hi_half(it * 2 + (U_PW1 + 3), 1, 1)

            def diagonals(it, c, n):
                act.wait_ge(g_u, it * 2 + 2)
                for k in range(n):
                    act.activation(DG[:, c, k, :], IDENT[:, :], ACT.Copy,
                                   scale=col("dw_w0", it * 2 + (8 * (TAPS - n + k) + c))).then_inc(g_d, 1)

            gate_unit(0)
            value_unit(0)
            with act.Fori(0, 3) as it:
                for c in range(2):
                    diagonals(it, c, TAPS_PE)
                    (gate_unit, value_unit)[c](it + 1)
            for c in range(2):
                diagonals(3, c, TAPS_PE_LAST)
            act.wait_ge(s_ss, ST_MEAN + 1)
            act.activation(R[:, :], PS_[:, ST_BANK, :], ACT.Copy, scale=1.0 / D).then_inc(n_m, 1)
            act.wait_ge(n_m, 1)
            act.activation(sc_(S_DUMP + 1), sc_(S_EPS), ACT.Copy).then_inc(s_ln, 1)
            act.activation(sc_(S_DUMP + 2), sc_(S_EPS), ACT.Copy).then_inc(s_r, 1)
            for c in range(DC):
                square(ST_VAR, c, CV[:, c, :])
            rms(ST_VAR, 1.0 / D)
            for c in range(DC):
                act.wait_ge(n_t, c + 1)
                act.activation(TF[:, c % 2, :], TA[:, c % 2, :], ACT.Silu, scale=col("ln_g", c), bias=col("ln_b", c)
                               ).then_inc(n_a, 1)
                act.wait_ge(n_a, c + 1)
                act.activation(XH[:, c, :], TF[:, c % 2, :], ACT.Copy).then_inc(n_h, 1)
            for u in range(U_PW2, U_PW2 + 4):
                if u < U_PW2 + 3:
                    hi_half(u + 2, u % 2, 0)
                    hi_half(u + 2, u % 2, 1)
                for c in range(2):
                    n = 2 * (u - U_PW2) + c
                    square(ST_F1, n, X[:, n, :])
            rms(ST_F1, 1.0 / D)
            split(5, "ffn_norm", 8)
            prep_late(U_FFN[1] + 1)
            feed_forward(1, None)
            for b in range(TB):
                act.wait_ge(s_yt, 2 * b + 2)
                act.activation(XROW[:, b, T:D], PS_[:, (2 * b + 1) % 4, :], ACT.Copy).then_inc(s_yc[1], 1)

        @block.vector
        def _(dve):
            tt, stt = dve.tensor_tensor, dve.scalar_tensor_tensor

            def lo_half(u, j, half, kn=8):
                dve.wait_ge(s_hi, u * 2 + (half + 1))
                a, b = (0, 4) if half == 0 else (4, kn)
                tt(WL[:, j, a:b, :], RAW[:, j, a:b, :], WH[:, j, a:b, :].bitcast(F32), ALU.subtract).then_inc(s_lo, 1)

            def prep_late(u):
                lo_half(u, 1, 0)
                lo_half(u, 1, 1)

            def clear_sum(stat):
                dve.memset(SQ[:, :], 0.0).then_inc(s_sqa, 1)

            def add_square(stat, m):
                dve.wait_ge(s_sqr, 8 * squares(stat) + m + 1)
                dve.wait_ge(s_sqa, 9 * stat + 1 + m)
                tt(SQ[:, :], SQ[:, :], TF[:, m % 2, :], ALU.add).then_inc(s_sqa, 1)

            def banks(j, c):
                return PS_[:, 2 * j + c, :]

            def mod_unit(a):
                dve.wait_ge(s_ar[a % 2], 16 * (a // 2 + 1))
                dst = MACC[:, a * UW:a * UW + UW]
                for k in range(8):
                    w, s = ARAW[:, a % 2, k, :], sc_(S_CS + k)
                    if k == 0:
                        dve.tensor_scalar(dst, w, s, None, ALU.mult).then_inc(s_as, 1)
                        continue
                    dve.wait_ge(s_as, 7 * (summed(a)[0] - 1) + k)
                    stt(dst, w, s, dst, ALU.mult, ALU.add).then_inc(s_as if k < 7 else s_ad, 1)

            def split(m, gs=None, gain=None, k=0):
                dve.wait_ge(s_r, (ST_X0, ST_X1, ST_X2, ST_F0, ST_X3, ST_F1)[m] + 1)

                def scaled(c):
                    tt(TA[:, c % 2, :], X[:, c, :], R[:, :], ALU.mult).then_inc(sp_t, 1)

                scaled(0)
                scaled(1)
                for c in range(DC):
                    dve.wait_ge(sp_h, 8 * m + c + 1)
                    if gain is None:
                        tt(XL[:, c, :], TF[:, c % 2, :], XH[:, c, :].bitcast(F32), ALU.subtract).then_inc(s_x, 1)
                    else:
                        stt(XL[:, c, :], TA[:, c % 2, :], col(gain, k + c), XH[:, c, :].bitcast(F32), ALU.mult,
                            ALU.subtract).then_inc(s_x, 1)
                    if c + 2 < DC:
                        if gain is not None:
                            dve.wait_ge(s_x, (0, 8, 16, 32, 40, 56)[m] + c + 1)
                        scaled(c + 2)

            def post_norm(stat, nth, gate):
                dve.wait_ge(s_r, stat + 1)
                clear_sum(stat + 1)
                tt(TA[:, 0, :], Y[:, 0, :], R[:, :], ALU.mult).then_inc(s_pn, 1)
                for c in range(DC):
                    if c + 1 < DC:
                        if c >= 1:
                            dve.wait_ge(s_xu, 8 * squares(stat + 1) + c)
                        tt(TA[:, (c + 1) % 2, :], Y[:, c + 1, :], R[:, :], ALU.mult).then_inc(s_pn, 1)
                    dve.wait_ge(s_pn, 8 * nth + c + 1)
                    stt(X[:, c, :], TA[:, c % 2, :], sc_(gate + c), X[:, c, :], ALU.mult, ALU.add).then_inc(s_xu, 1)
                    if c >= 1:
                        add_square(stat + 1, c - 1)
                add_square(stat + 1, DC - 1)

            def residual_window(u, j, n, stat=None, dst=X, first=False, prep=True):
                dve.wait_ge(s_mm, u + 1)
                for c in range(2):
                    d = dst[:, ds(n + c, 1), :] if not isinstance(n, int) else dst[:, n + c:n + c + 1, :]
                    src = PS_[:, 2 * j + c:2 * j + c + 1, :]
                    ins = dve.tensor_copy(d, src) if first else tt(d, src, d, ALU.add)
                    if stat is not None:
                        ins.then_inc(s_xu, 1)
                    elif c == 1:
                        ins.then_inc(s_ev, 1)
                if stat is not None:
                    dve.wait_ge(s_xu, 8 * squares(stat) + n + 2)
                    dve.tensor_copy(sc_(S_DUMP), sc_(S_EPS)).then_inc(s_ev, 1)
                if prep and not (stat is not None and n == 6):
                    lo_half(u + 2, j, 0)
                    lo_half(u + 2, j, 1)
                if stat is not None:
                    add_square(stat, n)
                    add_square(stat, n + 1)

            for t in range(VT):
                n = TILE_ROWS[t]
                dve.wait_ge(s_vt, t + 1)
                dve.tensor_copy(VCOL[:, TILE_COL[t]:TILE_COL[t] + n], PS_[:, 6 + t % 2, 0:n]).then_inc(s_ve, 1)
                if t == 0:
                    dve.wait_ge(s_const, 7)
                    clear_sum(ST_X0)
                    dve.wait_ge(s_cs, 1)
                    mod_unit(0)
                    for c in range(DC):
                        dve.wait_ge(s_xt, c + 1)
                        dve.tensor_copy(X[:, c, :], PS_[:, c % 4, :]).then_inc(s_xe, 1)
                        dve.wait_ge(s_xe, c + 1)
                        dve.tensor_copy(sc_(S_DUMP), sc_(S_EPS)).then_inc(s_xu, 1)
                        if c >= 1:
                            add_square(ST_X0, c - 1)
                    add_square(ST_X0, DC - 1)
            for a in (2, 4, 6):
                mod_unit(a)
            for u in range(2):
                lo_half(u, u, 0)
                lo_half(u, u, 1)
            dve.wait_ge(s_ac, 1)
            tt(sc_(S_MOD, 16), PS_[:, COL_BANK, 0:16], col("ada_b", 0, 16), ALU.add).then_inc(s_sm, 1)
            dve.wait_ge(s_sm, 1)
            dve.wait_ge(s_ve, VT)
            stt(sc_(S_GS0, 8), sc_(S_MOD + 8, 8), 1.0, col("gains", 0, 8), ALU.add, ALU.mult).then_inc(s_sm, 1)
            dve.tensor_scalar(sc_(S_Q8), col("q_g"), -DH ** -0.5, None, ALU.mult).then_inc(s_sm, 1)
            split(0)

            for u in range(12):
                step, j = u // 3, u % 2
                dve.wait_ge(s_mm, u + 1)
                if u % 3 == 0:
                    dve.tensor_copy(TF[:, 0, :], banks(j, 0))
                    dve.tensor_copy(TF[:, 1, :], banks(j, 1)).then_inc(s_ev, 1)
                elif u % 3 == 1:
                    dve.wait_ge(s_ev, u)
                    for c in range(2):
                        tt(ZP[:, c, 1:T + 1], banks(j, c), TF[:, c, :], ALU.mult).then_inc(c_z, 1)
                    dve.wait_ge(c_z, 2 * step + 2)
                    dve.tensor_copy(sc_(S_DUMP), sc_(S_EPS)).then_inc(s_ev, 1)
                    for tap, off in ((0, 0), (2, 2)):
                        for c in range(2):
                            n = 2 * step + c
                            if tap == 0:
                                dve.wait_ge(c_t, n + 1)
                            else:
                                dve.wait_ge(c_y, 4 * step + c + 1)
                            stt(TA[:, c, :], ZP[:, c, off:off + T], col("sc_conv", 8 * tap + n), TA[:, c, :],
                                ALU.mult, ALU.add).then_inc(c_y, 1)
                else:
                    for c in range(2):
                        dve.wait_ge(c_y, 4 * step + 3 + c)
                        tt(TA[:, c, :], banks(j, c), TA[:, c, :], ALU.mult).then_inc(c_g, 1)
                    dve.wait_ge(c_g, 2 * step + 2)
                    dve.tensor_copy(sc_(S_DUMP), sc_(S_EPS)).then_inc(s_ev, 1)
                lo_half(u + 2, j, 0)
                lo_half(u + 2, j, 1)
                if u % 3 == 2:
                    for c in range(2):
                        n = 2 * step + c
                        dve.wait_ge(c_h, n + 1)
                        tt(HL[:, n, :], TA[:, c, :], HH[:, n, :].bitcast(F32), ALU.subtract).then_inc(s_h, 1)
                for a in window_mods(u):
                    mod_unit(a)
            clear_sum(ST_Y0)
            for u in range(12, 16):
                residual_window(u, u % 2, 2 * (u - 12), ST_Y0, Y, first=True)
                if u == 14:
                    dve.wait_ge(s_ac, 2)
                    tt(sc_(S_MOD + 16, 32), PS_[:, COL_BANK, 16:48], col("ada_b", 16, 32), ALU.add).then_inc(s_sm, 1)
                    dve.wait_ge(s_sm, 4)
                    tt(sc_(S_MG0, 8), sc_(S_MOD + 16, 8), col("gains", 8, 8), ALU.mult).then_inc(s_sm, 1)
                    stt(sc_(S_GS1, 8), sc_(S_MOD + 32, 8), 1.0, col("gains", 16, 8), ALU.add, ALU.mult).then_inc(s_sm, 1)
                    tt(sc_(S_MG1, 8), sc_(S_MOD + 40, 8), col("gains", 24, 8), ALU.mult).then_inc(s_sm, 1)
                    dve.wait_ge(s_sm, 7)
            post_norm(ST_Y0, 0, S_MG0)
            split(1)
            prep_late(U_MLP + 1)

            for g in range(4):
                with dve.Fori(0, 2) as it:
                    for j in range(2):
                        u = it * 2 + (U_MLP + 8 * g + j)
                        dve.wait_ge(s_mm, u + 1)
                        for c in range(2):
                            dve.tensor_scalar(TA[:, c, :], banks(j, c), 0.0, None, ALU.max).then_inc(m_r, 1)
                        dve.wait_ge(m_r, it * 4 + (8 * g + 2 * j + 2))
                        dve.tensor_copy(sc_(S_DUMP), sc_(S_EPS)).then_inc(s_ev, 1)
                        lo_half(u + 2, j, 0)
                        lo_half(u + 2, j, 1)
                        for c in range(2):
                            n = it * 4 + (2 * j + c)
                            dve.wait_ge(m_h, it * 4 + (8 * g + 2 * j + c + 1))
                            tt(HL[:, ds(n, 1), :], TF[:, c:c + 1, :], HH[:, ds(n, 1), :].bitcast(F32), ALU.subtract
                               ).then_inc(s_h, 1)
                if g < 3:
                    with dve.Fori(0, 2) as it:
                        for j in range(2):
                            residual_window(it * 2 + (U_MLP + 8 * g + 4 + j), j, it * 4 + 2 * j, None, Y, first=g == 0)
            clear_sum(ST_Y1)
            for u in range(U_MLP + 28, U_MLP + 32):
                residual_window(u, u % 2, 2 * (u - U_MLP - 28), ST_Y1, Y)
            post_norm(ST_Y1, 1, S_MG1)
            dve.wait_ge(s_fh, 1)
            tt(FL[:, :, :], FRAW[:, :, :], FH[:, :, :].bitcast(F32), ALU.subtract).then_inc(s_fl, 1)
            split(2, gain="even_norm")
            prep_late(U_EVEN + 1)

            dve.wait_ge(s_vin2, 16)
            dve.wait_ge(s_f, 1)
            dve.tensor_scalar(CA[:, 1, 0:T], PS_[0:8, COL_BANK, :], small[0:8, S_BF:S_BF + 1], None, ALU.add
                              ).then_inc(e_f, 1)
            dve.wait_ge(e_a, 3)
            stt(TF[0:8, 1, :], CA[:, 1, 0:T], 0.0, CA[:, 0, 0:T], ALU.min, ALU.subtract).then_inc(e_c, 1)
            dve.wait_ge(e_c, 1)
            dve.memset(CA[:, :, 0:256], 0.0)
            dve.tensor_copy(CA[:, 0, 256:256 + T], TF[0:8, 1, :]).then_inc(e_c, 1)
            for n in range(9):
                dve.wait_ge(e_c, n + 2)
                a, b = n % 2, (n + 1) % 2
                tt(CA[:, b, 256:256 + T], CA[:, a, 256:256 + T], CA[:, a, 256 - 2 ** n:256 + T - 2 ** n], ALU.add
                   ).then_inc(e_c, 1)
            for u in range(U_EVEN, U_EVEN + 8):
                j, k = u % 2, u - U_EVEN
                dve.wait_ge(s_mm, u + 1)
                if k < 4:
                    for c in range(2):
                        dve.tensor_copy(QK[:, 2 * k + c, :], banks(j, c)).then_inc(e_q, 1)
                    dve.wait_ge(e_q, 2 * k + 2)
                    dve.tensor_copy(sc_(S_DUMP), sc_(S_EPS)).then_inc(s_ev, 1)
                elif k < 6:
                    for c in range(2):
                        ins = dve.tensor_copy(V[:, 2 * c:2 * c + 2, (k - 4) * UW:(k - 3) * UW],
                                              PS_[:, 2 * j + c, :].rearrange("p (b n) -> p b n", b=2))
                    ins.then_inc(s_ev, 1)
                else:
                    dve.wait_ge(s_zero, 1)
                    for c in range(2):
                        dve.tensor_copy(UP[:, 2 * (k - 6) + c, 16:], banks(j, c)).then_inc(e_u, 1)
                    dve.wait_ge(e_u, 2 * (k - 6) + 2)
                    dve.tensor_copy(sc_(S_DUMP), sc_(S_EPS)).then_inc(s_ev, 1)
                lo_half(u + 2, j, 0)
                lo_half(u + 2, j, 1)
                if k == 6:
                    dve.wait_ge(s_f, 1)
                    dve.memset(QS[64:97, :, :], 0.0).then_inc(s_zero, 1)
                    dve.memset(KS[64:97, :, :], 0.0).then_inc(s_zero, 1)
                    dve.wait_ge(s_zero, 3)
                    dve.memset(QS[96:97, :, :], 1.0)
                    dve.memset(KS[64:65, :, :], -1.0).then_inc(s_zero, 1)
            dve.wait_ge(e_r, 8)
            with dve.Fori(0, HEADS // 2) as pair:
                for h in range(2):
                    lo, hi = h * DH, h * DH + DH
                    stt(QS[0:DH, h:h + 1, :], QK[lo:hi, ds(pair, 1), :], small[lo:hi, S_Q8:S_Q8 + 1],
                        SQT[lo:hi, ds(pair, 1), :], ALU.mult, ALU.mult).then_inc(a_qk, 1)
                    stt(KS[0:DH, h:h + 1, :], QK[lo:hi, ds(pair + 4, 1), :], col("k_g")[lo:hi, :],
                        SQT[lo:hi, ds(pair + 4, 1), :], ALU.mult, ALU.mult).then_inc(a_qk, 1)
                for s in range(12):
                    if s < 8:
                        n = (s % 4 + 1) * P
                        dve.wait_ge(a_s, pair * 8 + (s + 1))
                        dve.tensor_reduce(sc_(S_MN + s), PS_[:, S_BANKS[s % 4], 0:n], AX.X, ALU.min).then_inc(a_min, 1)
                    if 2 <= s < 10:
                        dve.wait_ge(a_e, pair * 8 + (s - 1))
                        dve.reciprocal(sc_(S_RR + s - 2), sc_(S_RS + s - 2)).then_inc(a_rr, 1)
                    if s >= 4:
                        k = s - 4
                        dve.wait_ge(a_o, pair * 8 + (k + 1))
                        dve.wait_ge(a_rr, pair * 8 + (k + 1))
                        dve.tensor_scalar(OT[:, k % 4, ds(pair * P + k // 4 * DH, DH)], PS_[:, k % 2, 0:DH],
                                          sc_(S_RR + k), None, ALU.mult).then_inc(a_oe, 1)
            for c in range(4):
                dve.wait_ge(a_h, c + 1)
                tt(XL[:, c, :], PS_[:, c, :], XH[:, c, :].bitcast(F32), ALU.subtract).then_inc(s_x, 1)
            dve.wait_ge(e_w, WINDOW_STEPS)
            for g, w in enumerate(WINDOWS):
                stt(UP[:, g, 16:], PS[:, g, :], 1.0 / w, UP[:, g, 16:], ALU.mult, ALU.subtract).then_inc(e_mx, 1)
            for g in range(4):
                dve.wait_ge(e_ph, g + 1)
                stt(XL[:, 4 + g, :], PS_[:, 4 + g, :], col("pool_scale", g), XH[:, 4 + g, :].bitcast(F32),
                    ALU.mult, ALU.subtract).then_inc(s_x, 1)
            clear_sum(ST_F0)
            for u in range(U_EOUT, U_EOUT + 4):
                residual_window(u, u % 2, 2 * (u - U_EOUT), ST_F0)

            def feed_forward(layer, next_stat):
                u = U_FFN[layer]
                t0 = 4 * 11 * layer
                dve.memset(ZP[:, :, 0:2], 0.0)
                for first, steps, kn in GROUPS:
                    with dve.Fori(0, steps) as it:
                        for j, half in ((0, 0), (1, NG)):
                            dve.wait_ge(s_mm, it * 2 + (u + 1 + j))
                            z = it * 4 + (t0 + 4 * first + 2 * j)
                            if j == 1:
                                dve.wait_ge(f_y, it * 8 + (2 * t0 + 8 * first + 4))
                            for c in range(2):
                                dve.tensor_copy(ZP[:, c, 2:T + 2], banks(j, c)).then_inc(f_z, 1)
                            lo_half(it * 2 + (u + 2 + j), j, 0)
                            dve.wait_ge(f_z, z + 2)
                            dve.tensor_copy(sc_(S_DUMP), sc_(S_EPS)).then_inc(s_ev, 1)
                            for tap in (1, 0):
                                for c in range(2):
                                    y = it * 8 + (2 * t0 + 8 * first + 4 * j)
                                    if tap == 1:
                                        dve.wait_ge(f_t, z + c + 1)
                                    else:
                                        dve.wait_ge(f_y, y + c + 1)
                                    stt(TA[:, c, :], ZP[:, c, tap:tap + T],
                                        col(f"fw{layer}{tap}", it * 2 + (half + 2 * first + c)), TA[:, c, :],
                                        ALU.mult, ALU.add).then_inc(f_y, 1)
                            if j == 1:
                                for c in range(2):
                                    dve.wait_ge(f_y, y + 3 + c)
                                    dve.wait_ge(f_s, it * 2 + (t0 // 2 + 2 * first + c + 1))
                                    tt(TF[:, c, :], TF[:, c, :], TA[:, c, :], ALU.mult).then_inc(f_p, 1)
                            lo_half(it * 2 + (u + 2 + j), j, 1)
                            if j == 1:
                                for c in range(2):
                                    n = it * 2 + c
                                    dve.wait_ge(f_h, it * 2 + (t0 // 2 + 2 * first + c + 1))
                                    tt(HL[:, ds(n, 1), :], TF[:, c:c + 1, :], HH[:, ds(n, 1), :].bitcast(F32),
                                       ALU.subtract).then_inc(s_h, 1)
                    u += 2 * steps
                    if first + steps < 11:
                        with dve.Fori(0, 2) as it:
                            for j in range(2):
                                residual_window(it * 2 + (u + j), j, it * 4 + 2 * j)
                    else:
                        if next_stat is not None:
                            clear_sum(next_stat)
                        for v in range(u, u + 4):
                            residual_window(v, v % 2, 2 * (v - u), next_stat, prep=v + 2 < U_END)
                    u += 4

            split(3, gain="ffn_norm")
            prep_late(U_FFN[0] + 1)
            feed_forward(0, ST_X3)
            split(4, gain="odd_norm")
            prep_late(U_PW1 + 1)

            dve.memset(UPAD[:, :, 0:PADU], 0.0).then_inc(s_zero, 1)
            def pw1_window(it, j):
                u = it * 2 + (U_PW1 + j)
                dve.wait_ge(s_mm, u + 1)
                for c in range(2):
                    if j == 0:
                        dve.tensor_copy(TA[:, c, :], banks(j, c)).then_inc(g_c, 1)
                    else:
                        dve.wait_ge(g_s, it * 2 + (c + 1))
                        tt(UPAD[:, ds(it * 2 + c, 1), PADU:], PS_[:, 2 * j + c:2 * j + c + 1, :], TF[:, c:c + 1, :],
                           ALU.mult).then_inc(g_u, 1)
                dve.wait_ge(g_u if j else g_c, it * 2 + 2)
                dve.tensor_copy(sc_(S_DUMP), sc_(S_EPS)).then_inc(s_ev, 1)
                lo_half(u + 2, j, 0)
                lo_half(u + 2, j, 1)

            def taps(it, c, done, n):
                dst = CV[:, ds(it * 2 + c, 1), :]
                odd = R[:, :].rearrange("p (a t) -> p a t", a=1)
                for tap in range(n):
                    src = UPAD[:, ds(it * 2 + c, 1), tap:tap + T]
                    if tap == 0:
                        dve.tensor_scalar(dst, src, col("dw_w0", it * 2 + c), col("dw_b", it * 2 + c), ALU.mult,
                                          ALU.add).then_inc(g_v, 1)
                    elif tap == 1:
                        dve.tensor_scalar(odd, src, col("dw_w0", it * 2 + (8 * tap + c)), None, ALU.mult
                                          ).then_inc(g_v, 1)
                    else:
                        dve.wait_ge(g_v, done + (tap - 1))
                        acc = odd if tap % 2 else dst
                        stt(acc, src, col("dw_w0", it * 2 + (8 * tap + c)), acc, ALU.mult, ALU.add).then_inc(g_v, 1)
                dve.wait_ge(g_v, done + n)
                tt(dst, dst, odd, ALU.add).then_inc(g_o, 1)
                dve.wait_ge(g_o, it * 2 + (c + 1))
                dve.wait_ge(g_m, it * 2 + (c + 1))
                tt(dst, PS_[:, 6 + c:7 + c, :], dst, ALU.add).then_inc(g_a, 1)
                dve.wait_ge(g_a, it * 2 + (c + 1))
                dve.wait_ge(s_sqa, it * 2 + (9 * ST_MEAN + 1 + c))
                sq = SQ[:, :].rearrange("p (a t) -> p a t", a=1)
                tt(sq, sq, dst, ALU.add).then_inc(s_sqa, 1)

            clear_sum(ST_MEAN)
            pw1_window(0, 0)
            dve.wait_ge(s_zero, 5)
            pw1_window(0, 1)
            dve.wait_ge(g_u, 2)
            with dve.Fori(0, 3) as it:
                for c in range(2):
                    taps(it, c, it * (2 * (TAPS - TAPS_PE)) + c * (TAPS - TAPS_PE), TAPS - TAPS_PE)
                    pw1_window(it + 1, c)
            dve.wait_ge(g_u, 8)
            for c in range(2):
                taps(3, c, 6 * (TAPS - TAPS_PE) + c * (TAPS - TAPS_PE_LAST), TAPS - TAPS_PE_LAST)
            dve.wait_ge(n_m, 1)
            clear_sum(ST_VAR)
            for c in range(DC):
                tt(CV[:, c, :], CV[:, c, :], R[:, :], ALU.subtract).then_inc(s_xu, 1)
                if c >= 1:
                    add_square(ST_VAR, c - 1)
            add_square(ST_VAR, DC - 1)
            dve.wait_ge(s_r, ST_VAR + 1)

            def normed(c):
                tt(TA[:, c % 2, :], CV[:, c, :], R[:, :], ALU.mult).then_inc(n_t, 1)

            normed(0)
            normed(1)
            for c in range(DC):
                dve.wait_ge(n_h, c + 1)
                tt(XL[:, c, :], TF[:, c % 2, :], XH[:, c, :].bitcast(F32), ALU.subtract).then_inc(s_x, 1)
                if c + 2 < DC:
                    normed(c + 2)
            clear_sum(ST_F1)
            for u in range(U_PW2, U_PW2 + 4):
                residual_window(u, u % 2, 2 * (u - U_PW2), ST_F1)
            split(5, gain="ffn_norm", k=8)
            prep_late(U_FFN[1] + 1)
            feed_forward(1, None)
            for b in range(TB):
                dve.wait_ge(s_yt, 2 * b + 1)
                dve.tensor_copy(XROW[:, b, 0:T], PS_[:, (2 * b) % 4, :]).then_inc(s_yc[0], 1)

        @block.tensor
        def _(pe):
            def product(u, j, mh, ml, kn=8, ready=None, base_=0):
                if not (isinstance(u, int) and u < 2):
                    pe.wait_ge(s_ev, u - 1)
                for k in range(kn):
                    if k == 0 or k == 4:
                        pe.wait_ge(s_lo, u * 2 + (k // 4 + 1))
                    pe.wait_ge(ready, base_ + k + 1)
                    for c in range(2):
                        wh, wl = (w[:, j, k, c * P:c * P + P] for w in (WH, WL))
                        o = PS_[:, 2 * j + c, :]
                        pe.matmul(o, wh, mh[:, k, :], start=(k == 0), stop=False)
                        pe.matmul(o, wh, ml[:, k, :], start=False, stop=False)
                        mm = pe.matmul(o, wl, mh[:, k, :], start=False, stop=(k == kn - 1))
                mm.then_inc(s_mm, 1)

            def x_units(u0, n, base_):
                with pe.Fori(0, n // 2) as it:
                    for j in range(2):
                        product(it * 2 + (u0 + j), j, XH, XL, 8, s_x, base_)

            def h_units(u0, n, base_, kn=8):
                with pe.Fori(0, n // 2) as it:
                    for j in range(2):
                        product(it * 2 + (u0 + j), j, HH, HL, kn, s_h, base_)

            def channel_sum(stat):
                pe.wait_ge(s_sqa, 9 * stat + 9)
                if stat:
                    pe.wait_ge(s_r, stat)
                pe.matmul(PS_[:, ST_BANK, :], ONES[:, :], SQ[:, :], start=True, stop=True).then_inc(s_ss, 1)

            def mod_product(a):
                pe.wait_ge(s_ar[a % 2], 16 * (a // 2 + 1))
                pe.wait_ge(s_cs, 1)
                for n in range(2):
                    for k in range(8):
                        mm = pe.matmul(PS_[:, COL_BANK, 2 * a + n:2 * a + n + 1], ARAW[:, a % 2, k, n * P:n * P + P],
                                       sc_(S_CS + k), start=(k == 0), stop=(k == 7))
                mm.then_inc(s_ap, 1)

            pe.wait_ge(s_const, 7)
            pe.wait_ge(s_vin0, 16 * 4)
            for t in range(VT):
                n = TILE_ROWS[t]
                if t == 1:
                    pe.wait_ge(s_vin, 16 * (7 + 4 + 2 + 8))
                if t >= 2:
                    pe.wait_ge(s_ve, t - 1)
                pe.transpose(PS_[:, 6 + t % 2, 0:n], VROW[0:n, t, :], IDENT[0:n, 0:n]).then_inc(s_vt, 1)
                if t == 0:
                    pe.wait_ge(s_xin, 16)
                    for c in range(DC):
                        if c >= 4:
                            pe.wait_ge(s_xe, c - 3)
                        for b in range(TB):
                            tr = pe.transpose(PS_[:, c % 4, b * P:b * P + P], XROW[:, b, c * P:c * P + P], IDENT[:, :])
                        tr.then_inc(s_xt, 1)
                    mod_product(1)
                    channel_sum(ST_X0)
            for a in (3, 5, 7):
                mod_product(a)
            pe.wait_ge(s_ad, 4)
            for n in (0, 1, 4, 5, 8, 9, 12, 13):
                mm = pe.matmul(PS_[:, COL_BANK, n:n + 1], MACC[:, n * P:n * P + P], ONES[:, 0:1], start=True, stop=True)
            mm.then_inc(s_ac, 1)
            pe.wait_ge(s_xe, 8)
            for u in range(12):
                product(u, u % 2, XH, XL, 8, s_x, 0)
            for u in range(12, 16):
                if u == 14:
                    pe.wait_ge(s_ad, 20)
                    pe.wait_ge(s_sm, 1)
                    for n in range(16, 48):
                        mm = pe.matmul(PS_[:, COL_BANK, n:n + 1], MACC[:, n * P:n * P + P], ONES[:, 0:1], start=True,
                                       stop=True)
                    mm.then_inc(s_ac, 1)
                product(u, u % 2, HH, HL, 8, s_h, 0)
            channel_sum(ST_Y0)
            channel_sum(ST_X1)
            for g in range(4):
                x_units(U_MLP + 8 * g, 4, 8)
                h_units(U_MLP + 8 * g + 4, 4, 8 + 8 * g)
            channel_sum(ST_Y1)
            channel_sum(ST_X2)
            pe.wait_ge(s_fl, 1)
            pe.wait_ge(s_sm, 4)
            for k in range(8):
                pe.wait_ge(s_x, 16 + k + 1)
                o = PS_[:, COL_BANK, :]
                pe.matmul(o, FH[:, k, :], XH[:, k, :], start=(k == 0), stop=False)
                pe.matmul(o, FH[:, k, :], XL[:, k, :], start=False, stop=False)
                mm = pe.matmul(o, FL[:, k, :], XH[:, k, :], start=False, stop=(k == 7))
            mm.then_inc(s_f, 1)
            x_units(U_EVEN, 4, 16)
            def head_sums(n0):
                for n in (n0, n0 + 1):
                    pe.wait_ge(e_sq, n + 1)
                    if n >= 2:
                        pe.wait_ge(e_ln, n - 1)
                    pe.matmul(PS_[:, 6 + n % 2, :], BD[:, :], SQT[:, n, :], start=True, stop=True).then_inc(s_hn, 1)

            for j in range(2):
                u = U_EVEN + 4 + j
                pe.wait_ge(s_ev, u - 1)
                pe.wait_ge(s_lo, 2 * u + 2)
                for b in range(TB):
                    o = PS_[:, 2 * j + b // 2, b % 2 * UW:b % 2 * UW + UW]
                    for k in range(8):
                        xh, xl = (x[:, k, b * P:b * P + P] for x in (XH, XL))
                        pe.matmul(o, xh, WH[:, j, k, :], start=(k == 0), stop=False)
                        pe.matmul(o, xl, WH[:, j, k, :], start=False, stop=False)
                        mm = pe.matmul(o, xh, WL[:, j, k, :], start=False, stop=(k == 7))
                mm.then_inc(s_mm, 1)
                head_sums(2 * j)
            for j in range(2):
                product(U_EVEN + 6 + j, j, XH, XL, 8, s_x, 16)
                head_sums(4 + 2 * j)
            pe.wait_ge(s_zero, 4)
            pe.wait_ge(e_r, 8)
            pe.wait_ge(s_ev, U_EVEN + 8)
            with pe.Fori(0, HEADS // 2) as pair:
                for s in range(11):
                    if s < 8:
                        h, qb, n = s // 4, s % 4, (s % 4 + 1) * P
                        pe.wait_ge(a_qk, pair * 4 + (2 * h + 2))
                        pe.wait_ge(a_row, pair * 4 + (2 * h + 2))
                        if s >= 4:
                            pe.wait_ge(a_e, pair * 8 + (s - 3))
                        bank = PS_[:, S_BANKS[s % 4], :]
                        pe.matmul(bank[:, 0:n], QS[:, h, qb * P:qb * P + P], KS[:, h, 0:n], start=True, stop=True)
                        pe.matmul(bank[:, n - P:n], IDENT[:, :], MASK[:, :], start=False, stop=True,
                                  skip_group_check=True).then_inc(a_s, 1)
                    if 2 <= s < 10:
                        k = s - 2
                        pe.wait_ge(a_e, pair * 8 + (k + 1))
                        if k >= 2:
                            pe.wait_ge(a_tc, pair * 8 + (k - 1))
                        for b in range(k % 4 + 1):
                            tr = pe.transpose(PS_[:, 4 + k % 2, b * P:b * P + P], PR[:, k % 2, b * P:b * P + P], IDENT[:, :])
                        tr.then_inc(a_t, 1)
                    if s >= 3:
                        k = s - 3
                        pe.wait_ge(a_tc, pair * 8 + (k + 1))
                        if k >= 2:
                            pe.wait_ge(a_oe, pair * 8 + (k - 1))
                        for b in range(k % 4 + 1):
                            mm = pe.matmul(PS_[:, k % 2, 0:DH], PT[:, k % 2, b * P:b * P + P],
                                           V[:, b, ds(pair * P + k // 4 * DH, DH)], start=(b == 0), stop=(b == k % 4))
                        mm.then_inc(a_o, 1)
            pe.wait_ge(a_oe, 32)
            for c in range(4):
                for b in range(TB):
                    pe.transpose(PS_[:, c, b * P:b * P + P], OT[:, b, c * P:c * P + P], IDENT[:, :]).then_inc(a_ot, 1)
            pe.wait_ge(s_wp, 16)
            for g in range(4):
                pe.wait_ge(e_mx, g + 1)
                pe.matmul(PS_[:, 4 + g, :], WP[:, g, :], UP[:, g, 16:], start=True, stop=True).then_inc(s_pm, 1)
            pe.wait_ge(s_x, 28)
            x_units(U_EOUT, 4, 24)
            channel_sum(ST_F0)

            def feed_forward(layer):
                u, h = U_FFN[layer], 40 + 22 * layer
                for first, steps, kn in GROUPS:
                    x_units(u, 2 * steps, 32 if layer == 0 else 56)
                    h_units(u + 2 * steps, 4, h + 2 * first, kn)
                    u += 2 * steps + 4

            feed_forward(0)
            channel_sum(ST_X3)
            def taps(it, c, first, n):
                pe.wait_ge(g_u, it * 2 + 2)
                for k in range(n):
                    pe.wait_ge(g_d, first + (k + 1))
                    tap = TAPS - n + k
                    mm = pe.matmul(PS_[:, 6 + c, :], DG[:, c, k, :],
                                   UPAD[:, ds(it * 2 + c, 1), tap:tap + T].rearrange("p a t -> p (a t)"),
                                   start=(k == 0), stop=(k == n - 1))
                mm.then_inc(g_m, 1)

            for j in range(2):
                product(U_PW1 + j, j, XH, XL, 8, s_x, 40)
            with pe.Fori(0, 3) as it:
                for c in range(2):
                    product(it * 2 + (U_PW1 + 2 + c), c, XH, XL, 8, s_x, 40)
                    taps(it, c, it * (2 * TAPS_PE) + c * TAPS_PE, TAPS_PE)
            for c in range(2):
                taps(3, c, 6 * TAPS_PE + c * TAPS_PE_LAST, TAPS_PE_LAST)
            channel_sum(ST_MEAN)
            channel_sum(ST_VAR)
            x_units(U_PW2, 4, 48)
            channel_sum(ST_F1)
            feed_forward(1)
            pe.wait_ge(s_ev, U_END)
            for n in range(2 * TB):
                if n >= 4:
                    pe.wait_ge(s_yc[n % 2], n // 2 - 1)
                for c in range(4):
                    tr = pe.transpose(PS_[:, n % 4, c * P:c * P + P], X[:, n % 2 * 4 + c, n // 2 * P:n // 2 * P + P],
                                      IDENT[:, :])
                tr.then_inc(s_yt, 1)


_INS = ["x", "c", "ada_w", "ada_b", "norm_gains", "mlp_w_in", "mlp_w_out", "sc_w_in", "sc_conv", "sc_w_out",
        "even_norm_g_2", "even_w_in_2", "even_b_f_2", "even_q_norm_g_2", "even_k_norm_g_2", "even_w_pool_2",
        "even_pool_scale_2", "even_w_out_2", "odd_norm_g_2", "odd_w_pw1_2", "odd_dw_w_2", "odd_dw_b_2",
        "odd_ln_g_2", "odd_ln_b_2", "odd_w_pw2_2", "ffn_norm_g_2", "ffn_w_up_2", "ffn_conv_w_2",
        "ffn_conv_b_2", "ffn_w_down_2"]


def kernel(**inputs):
    import numpy as _np
    import concourse.bacc as _bacc
    from concourse.bass_utils import run_bass_kernel_spmd as _run

    nc = _bacc.Bacc("TRN2", target_bir_lowering=False, num_devices=1)
    arrays, args = {}, {}
    for name in _INS:
        a = _np.ascontiguousarray(inputs[name])
        arrays[f"in_{name}"] = a
        args[name] = nc.dram_tensor(f"in_{name}", a.shape, mybir.dt.from_np(a.dtype), kind="ExternalInput").ap()
    out = nc.dram_tensor("out", (1, T, D), F32, kind="ExternalOutput").ap()
    program(nc, args, out)
    r = _run(nc, [arrays], core_ids=[0])
    return r.results[0]["out"]
```
